# Optimizing a Trainium2 kernel written in Bass

```python
import jax, jax.numpy as jnp
from jax import lax
import numpy as np
import math

D_MODEL = 1024
BATCH = 1
SEQ = 256
DEPTH = 2

CHUNK = 64
Q_BLOCK = 128
PLE_DIM = 256
D_FF = 2816
CONV_DIM = 512
CONV_GROUPS = 8
CONV_K = 3
N_HEADS = 8
NOPE_DIM = 128
ROPE_DIM = 64
V_DIM = 128
Q_LORA = 384
KV_LORA = 256
ROPE_THETA = 10000.0
EPS = 1e-6
QK_DIM = NOPE_DIM + ROPE_DIM
ATTN_SCALE = QK_DIM ** -0.5
IN_SPLITS = (CONV_DIM, CONV_DIM, CONV_DIM, Q_LORA, KV_LORA, ROPE_DIM, D_MODEL, D_MODEL)
IN_COLS = sum(IN_SPLITS)


def rmsnorm(x, g):
    xf = x.astype(jnp.float32)
    y = xf * lax.rsqrt(jnp.mean(xf * xf, axis=-1, keepdims=True) + EPS)
    return (y * g.astype(jnp.float32)).astype(x.dtype)

def swiglu(x, w_gu, w_down):
    g, u = jnp.split(x @ w_gu, 2, axis=-1)
    return (jax.nn.silu(g) * u) @ w_down

def rope_tables(positions):
    inv_freq = ROPE_THETA ** (-jnp.arange(0, ROPE_DIM, 2, dtype=jnp.float32) / ROPE_DIM)
    ang = positions.astype(jnp.float32)[..., None] * inv_freq
    return jnp.cos(ang), jnp.sin(ang)

def apply_rope(x, cos, sin):
    half = ROPE_DIM // 2
    xf = x.astype(jnp.float32)
    x1, x2 = xf[..., :half], xf[..., half:]
    return jnp.concatenate([x1 * cos - x2 * sin, x2 * cos + x1 * sin], axis=-1).astype(x.dtype)

def short_conv_branch(b_gate, c_gate, v, conv_w, w_conv_out):
    seq = v.shape[1]
    z = c_gate * v
    zp = jnp.pad(z, ((0, 0), (CONV_K - 1, 0), (0, 0)))
    y = conv_w[0] * zp[:, 0:seq]
    for j in range(1, CONV_K):
        y = y + conv_w[j] * zp[:, j:j + seq]
    return (b_gate * y) @ w_conv_out

def block_causal_attention(q_nope, q_rope, k_nope, k_rope, v):
    seq = q_nope.shape[1]
    outs = []
    for i in range(seq // Q_BLOCK):
        q0, q1 = i * Q_BLOCK, (i + 1) * Q_BLOCK
        kn, kr, vb = k_nope[:, :q1], k_rope[:, :q1], v[:, :q1]
        s = (jnp.einsum('bqhd,bkhd->bhqk', q_nope[:, q0:q1], kn)
             + jnp.einsum('bqhd,bkd->bhqk', q_rope[:, q0:q1], kr)).astype(jnp.float32) * ATTN_SCALE
        q_chunk = (q0 + jnp.arange(Q_BLOCK)) // CHUNK
        k_chunk = jnp.arange(q1) // CHUNK
        mask = k_chunk[None, :] <= q_chunk[:, None]
        s = jnp.where(mask, s, -1e30)
        pr = jax.nn.softmax(s, axis=-1).astype(v.dtype)
        outs.append(jnp.einsum('bhqk,bkhd->bqhd', pr, vb))
    return jnp.concatenate(outs, axis=1)

def mla_branch(q_c, kv_c, k_r, q_norm_g, kv_norm_g, w_uq, w_ukv, w_mla_out, cos, sin):
    b, s, _ = q_c.shape
    q = (rmsnorm(q_c, q_norm_g) @ w_uq).reshape(b, s, N_HEADS, QK_DIM)
    q_nope = q[..., :NOPE_DIM]
    q_rope = apply_rope(q[..., NOPE_DIM:], cos[:, :, None, :], sin[:, :, None, :])
    kv = (rmsnorm(kv_c, kv_norm_g) @ w_ukv).reshape(b, s, N_HEADS, NOPE_DIM + V_DIM)
    k_nope, v = kv[..., :NOPE_DIM], kv[..., NOPE_DIM:]
    k_rope = apply_rope(k_r, cos, sin)
    o = block_causal_attention(q_nope, q_rope, k_nope, k_rope, v)
    return o.reshape(b, s, N_HEADS * V_DIM) @ w_mla_out

def first_inputs(seed: int = 0) -> dict:
    key = jax.random.key(seed)
    ks = jax.random.split(key, 24)
    f32 = jnp.float32

    def w(k, shape, fan_in):
        return jax.random.normal(k, shape, f32) * (fan_in ** -0.5)

    def gain(k, shape):
        return 1.0 + 0.05 * jax.random.normal(k, shape, f32)

    x = jax.random.normal(ks[0], (BATCH, SEQ, D_MODEL), f32)
    p = jax.random.normal(ks[1], (DEPTH, BATCH, SEQ, PLE_DIM), f32)
    offset = jax.random.randint(ks[2], (BATCH, 1), 0, 4096, dtype=jnp.int32)
    positions = offset + jnp.arange(SEQ, dtype=jnp.int32)[None, :]
    return {
        "x": x,
        "p": p,
        "positions": positions,
        "ffn1_norm": gain(ks[3], (DEPTH, D_MODEL)),
        "ffn1_w_gu": w(ks[4], (DEPTH, D_MODEL, 2 * D_FF), D_MODEL),
        "ffn1_w_down": w(ks[5], (DEPTH, D_FF, D_MODEL), D_FF),
        "mix_norm": gain(ks[6], (DEPTH, D_MODEL)),
        "w_in": w(ks[7], (DEPTH, D_MODEL, IN_COLS), D_MODEL),
        "conv_w": w(ks[8], (DEPTH, CONV_K, CONV_DIM), CONV_K),
        "w_conv_out": w(ks[9], (DEPTH, CONV_DIM, D_MODEL), CONV_DIM),
        "q_norm": gain(ks[10], (DEPTH, Q_LORA)),
        "kv_norm": gain(ks[11], (DEPTH, KV_LORA)),
        "w_uq": w(ks[12], (DEPTH, Q_LORA, N_HEADS * QK_DIM), Q_LORA),
        "w_ukv": w(ks[13], (DEPTH, KV_LORA, N_HEADS * (NOPE_DIM + V_DIM)), KV_LORA),
        "w_mla_out": w(ks[14], (DEPTH, N_HEADS * V_DIM, D_MODEL), N_HEADS * V_DIM),
        "w_o": w(ks[15], (DEPTH, D_MODEL, D_MODEL), D_MODEL),
        "ffn2_norm": gain(ks[16], (DEPTH, D_MODEL)),
        "ffn2_w_gu": w(ks[17], (DEPTH, D_MODEL, 2 * D_FF), D_MODEL),
        "ffn2_w_down": w(ks[18], (DEPTH, D_FF, D_MODEL), D_FF),
        "ple_norm": gain(ks[19], (DEPTH, D_MODEL)),
        "w_ple_gate": w(ks[20], (DEPTH, D_MODEL, D_MODEL), D_MODEL),
        "w_ple_proj": w(ks[21], (DEPTH, PLE_DIM, D_MODEL), PLE_DIM),
        "final_norm": gain(ks[22], (D_MODEL,)),
    }

def first_block(x, p, positions, ffn1_norm, ffn1_w_gu, ffn1_w_down, mix_norm, w_in, conv_w,
              w_conv_out, q_norm, kv_norm, w_uq, w_ukv, w_mla_out, w_o, ffn2_norm, ffn2_w_gu,
              ffn2_w_down, ple_norm, w_ple_gate, w_ple_proj, final_norm):
    cos, sin = rope_tables(positions)
    split_pts = list(np.cumsum(IN_SPLITS)[:-1])
    h = x
    for i in range(DEPTH):
        h = h + 0.5 * swiglu(rmsnorm(h, ffn1_norm[i]), ffn1_w_gu[i], ffn1_w_down[i])

        u = rmsnorm(h, mix_norm[i])
        b_g, c_g, v_c, q_c, kv_c, k_r, g_conv, g_mla = jnp.split(u @ w_in[i], split_pts, axis=-1)
        y_conv = short_conv_branch(b_g, c_g, v_c, conv_w[i], w_conv_out[i])
        y_mla = mla_branch(q_c, kv_c, k_r, q_norm[i], kv_norm[i], w_uq[i], w_ukv[i],
                           w_mla_out[i], cos, sin)
        merged = jax.nn.sigmoid(g_conv) * y_conv + jax.nn.sigmoid(g_mla) * y_mla
        h = h + merged @ w_o[i]

        h = h + 0.5 * swiglu(rmsnorm(h, ffn2_norm[i]), ffn2_w_gu[i], ffn2_w_down[i])

        gate = jax.nn.sigmoid(rmsnorm(h, ple_norm[i]) @ w_ple_gate[i])
        h = h + gate * (p[i] @ w_ple_proj[i])
    return rmsnorm(h, final_norm)


HEAD_DIM = 64
ATTN_WIDTH = D_MODEL // 2
ATTN_HEADS = ATTN_WIDTH // HEAD_DIM
KV_HEADS = 2
GROUP = ATTN_HEADS // KV_HEADS
IDX_HEADS = 16
IDX_DIM = 64
INDEX_TOPK = 256
CONV_WIDTH = D_MODEL // 4
CONV_KERNEL = 31
POOL_WIDTH = D_MODEL // 4
POOL_GROUPS = 4
POOL_GROUP_DIM = POOL_WIDTH // POOL_GROUPS
POOL_WINDOWS = (2, 4, 8, 16)
POOL_PAD = max(POOL_WINDOWS)
MIX_WIDTH = ATTN_WIDTH + CONV_WIDTH + POOL_WIDTH
D_FF_2 = 4 * D_MODEL
ROPE_THETA_2 = 500000.0
ROPE_DIM_2 = HEAD_DIM // 4
MAX_POS_OFFSET = 1024
NORM_EPS = 1e-6
LN_EPS = 1e-5

IN_SIZES = (
    ATTN_WIDTH,
    KV_HEADS * HEAD_DIM,
    KV_HEADS * HEAD_DIM,
    IDX_HEADS * IDX_DIM,
    IDX_DIM,
    IDX_HEADS,
    2 * CONV_WIDTH,
    POOL_WIDTH,
)
IN_WIDTH = int(sum(IN_SIZES))
IN_SPLITS_2 = [int(v) for v in np.cumsum(IN_SIZES)[:-1]]


def rmsnorm_2(x, g):
    xf = x.astype(jnp.float32)
    y = xf * lax.rsqrt(jnp.mean(xf * xf, axis=-1, keepdims=True) + NORM_EPS)
    return (y * g.astype(jnp.float32)).astype(x.dtype)

def layernorm(x, g, b):
    xf = x.astype(jnp.float32)
    mu = jnp.mean(xf, axis=-1, keepdims=True)
    var = jnp.mean(jnp.square(xf - mu), axis=-1, keepdims=True)
    y = (xf - mu) * lax.rsqrt(var + LN_EPS)
    return (y * g.astype(jnp.float32) + b.astype(jnp.float32)).astype(x.dtype)

def rope_tables_2(positions):
    inv_freq = ROPE_THETA_2 ** (-jnp.arange(0, ROPE_DIM_2, 2, dtype=jnp.float32) / ROPE_DIM_2)
    ang = positions.astype(jnp.float32)[..., None] * inv_freq
    return jnp.cos(ang)[:, :, None, :], jnp.sin(ang)[:, :, None, :]

def partial_rope(x, cos, sin):
    half = ROPE_DIM_2 // 2
    cos = cos.astype(x.dtype)
    sin = sin.astype(x.dtype)
    x1 = x[..., :half]
    x2 = x[..., half:ROPE_DIM_2]
    return jnp.concatenate([x1 * cos - x2 * sin, x2 * cos + x1 * sin, x[..., ROPE_DIM_2:]], axis=-1)

def dsa_sparse_attention(q, k, v, qi, ki, wi):
    B, S = q.shape[0], q.shape[1]
    n_blk = S // Q_BLOCK
    k_sel = min(INDEX_TOPK, S // 4)
    idx_scale = (IDX_DIM ** -0.5) * (IDX_HEADS ** -0.5)
    att_scale = HEAD_DIM ** -0.5
    neg = jnp.finfo(jnp.float32).min
    key_pos = jnp.arange(S)
    b_idx = jnp.arange(B)[:, None, None]
    ki_f = ki.astype(jnp.float32)

    def to_blocks(t):
        return jnp.moveaxis(t.reshape((B, n_blk, Q_BLOCK) + t.shape[2:]), 1, 0)

    q_b = to_blocks(q.reshape(B, S, KV_HEADS, GROUP, HEAD_DIM))
    qi_b = to_blocks(qi)
    wi_b = to_blocks(wi)
    t_b = key_pos.reshape(n_blk, Q_BLOCK)

    def block(args):
        q_blk, qi_blk, wi_blk, t_blk = args
        dots = jnp.einsum('bthd,bsd->bths', qi_blk.astype(jnp.float32), ki_f)
        idx = jnp.einsum('bths,bth->bts', jax.nn.relu(dots), wi_blk.astype(jnp.float32)) * idx_scale
        causal = key_pos[None, :] <= t_blk[:, None]
        idx = jnp.where(causal[None], idx, -jnp.inf)
        _, sel = lax.top_k(idx, k_sel)
        valid = sel <= t_blk[None, :, None]
        k_g = k[b_idx, sel]
        v_g = v[b_idx, sel]
        s = jnp.einsum('bthgd,btnhd->bthgn', q_blk, k_g).astype(jnp.float32) * att_scale
        s = jnp.where(valid[:, :, None, None, :], s, neg)
        pr = jax.nn.softmax(s, axis=-1).astype(v.dtype)
        o = jnp.einsum('bthgn,btnhd->bthgd', pr, v_g)
        return o.reshape(B, Q_BLOCK, ATTN_WIDTH)

    out = lax.map(block, (q_b, qi_b, wi_b, t_b))
    return jnp.moveaxis(out, 0, 1).reshape(B, S, ATTN_WIDTH)

def conformer_conv(u, conv_dw, conv_b, ln_g, ln_b, conv_pw):
    a, g = jnp.split(u, 2, axis=-1)
    y = a * jax.nn.sigmoid(g)
    y = lax.conv_general_dilated(
        y, conv_dw[:, None, :], window_strides=(1,), padding=[(CONV_KERNEL - 1, 0)],
        dimension_numbers=('NWC', 'WIO', 'NWC'), feature_group_count=CONV_WIDTH)
    y = y + conv_b
    y = jax.nn.silu(layernorm(y, ln_g, ln_b))
    return jnp.einsum('bsc,cd->bsd', y, conv_pw)

def multiscale_pool(u, pool_w, pool_scale):
    B, S, _ = u.shape
    uf = u.astype(jnp.float32)
    c = jnp.cumsum(uf, axis=1)
    c_pad = jnp.concatenate([jnp.zeros((B, POOL_PAD, POOL_WIDTH), jnp.float32), c], axis=1)
    t = jnp.arange(S)
    outs = []
    for gi, w in enumerate(POOL_WINDOWS):
        sl = slice(gi * POOL_GROUP_DIM, (gi + 1) * POOL_GROUP_DIM)
        win_sum = c[:, :, sl] - c_pad[:, POOL_PAD - w:POOL_PAD - w + S, sl]
        count = jnp.minimum(t + 1, w).astype(jnp.float32)[None, :, None]
        outs.append(win_sum / count - uf[:, :, sl])
    y = jnp.stack(outs, axis=2).astype(u.dtype)
    y = jnp.einsum('bsgc,gcd->bsgd', y, pool_w).reshape(B, S, POOL_WIDTH)
    return y * pool_scale

def second_inputs(seed: int = 0) -> dict:
    key = jax.random.key(seed)
    ks = jax.random.split(key, 24)
    nrm = jax.random.normal
    f32 = jnp.float32
    L = DEPTH
    x = nrm(ks[0], (BATCH, SEQ, D_MODEL), f32)
    p = nrm(ks[1], (DEPTH, BATCH, SEQ, PLE_DIM), f32)
    offs = jax.random.randint(ks[2], (BATCH, 1), 0, MAX_POS_OFFSET, dtype=jnp.int32)
    positions = (offs + jnp.arange(SEQ, dtype=jnp.int32)[None, :]).astype(jnp.int32)
    return {
        "x": x,
        "p": p,
        "positions": positions,
        "norm_mix_pre": 1.0 + 0.1 * nrm(ks[3], (L, D_MODEL), f32),
        "w_in": nrm(ks[4], (L, D_MODEL, IN_WIDTH), f32) * D_MODEL ** -0.5,
        "conv_dw": nrm(ks[5], (L, CONV_KERNEL, CONV_WIDTH), f32) * CONV_KERNEL ** -0.5,
        "conv_b": 0.02 * nrm(ks[6], (L, CONV_WIDTH), f32),
        "conv_ln_g": 1.0 + 0.1 * nrm(ks[7], (L, CONV_WIDTH), f32),
        "conv_ln_b": 0.02 * nrm(ks[8], (L, CONV_WIDTH), f32),
        "conv_pw": nrm(ks[9], (L, CONV_WIDTH, CONV_WIDTH), f32) * CONV_WIDTH ** -0.5,
        "pool_w": nrm(ks[10], (L, POOL_GROUPS, POOL_GROUP_DIM, POOL_GROUP_DIM), f32) * POOL_GROUP_DIM ** -0.5,
        "pool_scale": 1.0 + 0.1 * nrm(ks[11], (L, POOL_WIDTH), f32),
        "w_out": nrm(ks[12], (L, MIX_WIDTH, D_MODEL), f32) * MIX_WIDTH ** -0.5,
        "norm_mix_post": 1.0 + 0.1 * nrm(ks[13], (L, D_MODEL), f32),
        "norm_mlp_pre": 1.0 + 0.1 * nrm(ks[14], (L, D_MODEL), f32),
        "w_up": nrm(ks[15], (L, D_MODEL, D_FF_2), f32) * D_MODEL ** -0.5,
        "w_down": nrm(ks[16], (L, D_FF_2, D_MODEL), f32) * D_FF_2 ** -0.5,
        "norm_mlp_post": 1.0 + 0.1 * nrm(ks[17], (L, D_MODEL), f32),
        "ple_proj": nrm(ks[18], (L, PLE_DIM, D_MODEL), f32) * PLE_DIM ** -0.5,
        "ple_gate": nrm(ks[19], (L, D_MODEL, D_MODEL), f32) * D_MODEL ** -0.5,
    }

def second_block(x, p, positions, norm_mix_pre, w_in, conv_dw, conv_b, conv_ln_g, conv_ln_b,
              conv_pw, pool_w, pool_scale, w_out, norm_mix_post, norm_mlp_pre, w_up, w_down,
              norm_mlp_post, ple_proj, ple_gate):
    B, S, _ = x.shape
    cos, sin = rope_tables_2(positions)
    h = x
    for i in range(DEPTH):
        a = rmsnorm_2(h, norm_mix_pre[i])
        u = jnp.einsum('bsd,de->bse', a, w_in[i])
        q, k, v, qi, ki, wi, u_conv, u_pool = jnp.split(u, IN_SPLITS_2, axis=-1)
        q = partial_rope(q.reshape(B, S, ATTN_HEADS, HEAD_DIM), cos, sin)
        k = partial_rope(k.reshape(B, S, KV_HEADS, HEAD_DIM), cos, sin)
        v = v.reshape(B, S, KV_HEADS, HEAD_DIM)
        qi = partial_rope(qi.reshape(B, S, IDX_HEADS, IDX_DIM), cos, sin)
        ki = partial_rope(ki[:, :, None, :], cos, sin)[:, :, 0, :]
        y_attn = dsa_sparse_attention(q, k, v, qi, ki, wi)
        y_conv = conformer_conv(u_conv, conv_dw[i], conv_b[i], conv_ln_g[i],
                                conv_ln_b[i], conv_pw[i])
        y_pool = multiscale_pool(u_pool, pool_w[i], pool_scale[i])
        mix = jnp.concatenate([y_attn, y_conv, y_pool], axis=-1)
        mix = jnp.einsum('bse,ed->bsd', mix, w_out[i])
        h = h + rmsnorm_2(mix, norm_mix_post[i])
        m = rmsnorm_2(h, norm_mlp_pre[i])
        m = jnp.square(jax.nn.relu(jnp.einsum('bsd,df->bsf', m, w_up[i])))
        m = jnp.einsum('bsf,fd->bsd', m, w_down[i])
        h = h + rmsnorm_2(m, norm_mlp_post[i])
        gate = jax.nn.sigmoid(jnp.einsum('bsd,de->bse', h, ple_gate[i]))
        h = h + gate * jnp.einsum('bsp,pd->bsd', p[i], ple_proj[i])
    return h


def setup_inputs(seed=0):
    out = dict(first_inputs(seed))
    for name, value in second_inputs(seed + 1).items():
        if name != "x":
            out[name + "_2"] = value
    return out


def reference(
    x, p, positions, ffn1_norm, ffn1_w_gu, ffn1_w_down, mix_norm, w_in, conv_w, w_conv_out,
    q_norm, kv_norm, w_uq, w_ukv, w_mla_out, w_o, ffn2_norm, ffn2_w_gu, ffn2_w_down, ple_norm,
    w_ple_gate, w_ple_proj, final_norm, p_2, positions_2, norm_mix_pre_2, w_in_2, conv_dw_2,
    conv_b_2, conv_ln_g_2, conv_ln_b_2, conv_pw_2, pool_w_2, pool_scale_2, w_out_2,
    norm_mix_post_2, norm_mlp_pre_2, w_up_2, w_down_2, norm_mlp_post_2, ple_proj_2, ple_gate_2,
):
    x = first_block(
        x, p, positions, ffn1_norm, ffn1_w_gu, ffn1_w_down, mix_norm, w_in, conv_w, w_conv_out,
        q_norm, kv_norm, w_uq, w_ukv, w_mla_out, w_o, ffn2_norm, ffn2_w_gu, ffn2_w_down,
        ple_norm, w_ple_gate, w_ple_proj, final_norm,
    )
    return second_block(
        x, p_2, positions_2, norm_mix_pre_2, w_in_2, conv_dw_2, conv_b_2, conv_ln_g_2,
        conv_ln_b_2, conv_pw_2, pool_w_2, pool_scale_2, w_out_2, norm_mix_post_2,
        norm_mlp_pre_2, w_up_2, w_down_2, norm_mlp_post_2, ple_proj_2, ple_gate_2,
    )


_drawn_inputs = setup_inputs


def setup_inputs(seed=0):
    import zlib

    import numpy as np

    out = dict(_drawn_inputs(seed))
    spreads = {}
    factors = {'q_norm': 3.255, 'kv_norm': 2.881, 'conv_ln_b_2': 4.396}
    for name, (base, spread) in spreads.items():
        noise = np.random.default_rng([zlib.crc32(name.encode()), seed]).standard_normal(out[name].shape)
        drawn = base * np.exp(spread * noise) if base else spread * noise
        out[name] = __import__('jax').numpy.asarray(drawn.astype(out[name].dtype))
    for name, factor in factors.items():
        out[name] = (out[name] * factor).astype(out[name].dtype)
    return out
```

```python
import math
from contextlib import ExitStack

import numpy as np

import concourse.bass as bass
from concourse import mybir

F32 = mybir.dt.float32
F32R = mybir.dt.float32r
I32 = mybir.dt.int32
ALU = mybir.AluOpType
ACT = mybir.ActivationFunctionType
AX_X = mybir.AxisListType.X

P = 128
T = 256
TB = T // P
D = 1024
KD = D // P
NB = KD // 2
DEPTH = 2
F_FF = 2816
FF_STEPS = F_FF // 256
F_MLP = 4096
MLP_STEPS = F_MLP // 256
PLE = 256
RING = 3
CH = 2048
WORK = 4
EPS = 1e-6
LN_EPS = 1e-5
NEG = -1e30

CONV = 512
KV_COLS = 256
HEADS = 8
PAIRS = HEADS // 2
QK_DIM = 192
SCALE1 = QK_DIM ** -0.5
IN_B, IN_C, IN_V, IN_Q, IN_GC, IN_GM = 0, 512, 1024, 1536, 2240, 3264
CONV_K2 = 31
PAD2 = CONV_K2 - 1
POOL_PAD = 16
TOPK = 64
IDX_HEADS = 16
SCALE2 = 64 ** -0.5
IDX_SCALE = (64 ** -0.5) * (16 ** -0.5)
IN2_Q, IN2_KV, IN2_QI, IN2_KI, IN2_A, IN2_G, IN2_P = 0, 512, 768, 1792, 1872, 2128, 2384
TWO_PI = 6.283185307179586
TWO_PI_PARTS = (6.28125, math.floor((2 * math.pi - 6.28125) * 2 ** 22) / 2 ** 22)
TWO_PI_PARTS += (2 * math.pi - sum(TWO_PI_PARTS),)
PI_BELOW = 3.1415925
CAUSAL = -3.0e38
PICKED = -3.4028234663852886e38

V1_FFN1, V1_MIX, V1_FFN2, V1_PLE, V1_QN, V1_KVN, V1_CONV, V1_FINAL = 0, 8, 16, 24, 32, 35, 37, 49
V2_PRE, V2_MIXPOST, V2_MLPPRE, V2_MLPPOST, V2_DW, V2_CB, V2_LG, V2_LB, V2_PS = (
    0, 8, 16, 24, 32, 94, 96, 98, 100)

C_ID, C_R1, C_R2, C_ONES, C_MASK, C_RCNT, C_COL = 0, 128, 256, 384, 512, 896, 1408
C_WIDTH = C_COL + 4


def ffn_chunks(up, down, steps, pair):
    def ups(j):
        return [(up, 0, KD, g * F_FF + j * 256, 256) for g in range(2 if pair else 1)]
    out = ups(0)
    for j in range(1, steps):
        out += ups(j) + [(down, (j - 1) * 256, 2, 0, D)]
    return out + [(down, (steps - 1) * 256, 2, 0, D)]


def chunks_1():
    out = ffn_chunks("ffn1_w_gu", "ffn1_w_down", FF_STEPS, True)
    out += [("w_in", 0, KD, IN_Q + i * 256, 256) for i in range(3)]
    out += [("w_in", 0, KD, i * 256, 256) for i in range(6)]
    out += [("w_in", 0, KD, IN_GC + i * 256, 256) for i in range(4)]
    out += [("w_conv_out", 0, CONV // P, i * 256, 256) for i in range(4)]
    for hp in range(PAIRS):
        out += [("w_uq", 0, 3, hp * 384, 384), ("w_ukv", 0, 2, hp * 512, 512),
                ("w_in", 0, KD, IN_GM + hp * 256, 256)]
        if hp:
            out += [("w_mla_out", (hp - 1) * 256, 2, 0, D)]
    out += [("w_mla_out", (PAIRS - 1) * 256, 2, 0, D)]
    out += [("w_o", 0, KD, i * 256, 256) for i in range(4)]
    out += ffn_chunks("ffn2_w_gu", "ffn2_w_down", FF_STEPS, True)
    out += [("w_ple_proj", 0, 2, 0, D)]
    out += [("w_ple_gate", 0, KD, i * 256, 256) for i in range(4)]
    return out


def chunks_2():
    out = [("w_in_2", 0, KD, IN2_KI, 256)]
    out += [("w_in_2", 0, KD, IN2_QI + i * 256, 256) for i in range(4)]
    out += [("w_in_2", 0, KD, c, 256) for c in (IN2_KV, IN2_Q, IN2_Q + 256, IN2_A, IN2_G, IN2_P)]
    out += [("conv_pw_2", 0, 2, 0, 256)]
    out += [("w_out_2", 0, KD, i * 256, 256) for i in range(4)]
    out += ffn_chunks("w_up_2", "w_down_2", MLP_STEPS, False)
    out += [("ple_proj_2", 0, 2, i * 512, 512) for i in range(2)]
    out += [("ple_gate_2", 0, KD, i * 256, 256) for i in range(4)]
    return out


CHUNKS = {1: chunks_1(), 2: chunks_2()}
N1, N2 = len(CHUNKS[1]), len(CHUNKS[2])
assert N1 % RING == 0 and N2 % RING == 0

F1, A1, B1, C1, D1, E1 = 0, 33, 36, 42, 46, 50
W1 = 66
G1 = W1 + 4 + 33
KI2, PW2, WO2, M2 = 0, 11, 12, 16
G2 = M2 + 32

U1 = dict(vec=0, f1=1, a=23, b=26, c=33, d=37, e=41, w=85, f2=89, p=111, proj=112, gate=116)
UNITS1 = 120


def e_units():
    at, out = U1["e"], {}
    for hp in range(PAIRS):
        for name in ("qn", "qr", "k", "v", "rot"):
            out[name, hp] = at
            at += 1
        if hp:
            for name in ("pt0", "pt1", "o"):
                out[name, hp - 1] = at
                at += 1
        for name in ("gm", "sc0", "sc1"):
            out[name, hp] = at
            at += 1
    for name in ("pt0", "pt1", "o"):
        out[name, PAIRS - 1] = at
        at += 1
    assert at == U1["w"]
    return out


UE = e_units()


def units_2():
    names = ["vec", "ki", "wi0", "wi1", "rc", ("qi", 0), "rki", ("qi", 1), ("rqi", 0)]
    names += [("dot", 0, i) for i in range(3)]
    names += [("qi", 2), ("rqi", 1)] + [("dot", 1, i) for i in range(3)]
    names += [("qi", 3), ("rqi", 2)] + [("dot", 2, i) for i in range(3)]
    names += ["k", "v", ("rqi", 3)] + [("dot", 3, i) for i in range(3)]
    names += [("q", 0), "rk", ("q", 1), ("rq", 0), "a", ("rq", 1), "g", "pool", "poolw", "pw"]
    for h in range(HEADS):
        names += [("sc", h)]
        if h:
            names += [("pt", h - 1)]
        if h >= 2 and h % 2 == 0:
            names += [("o", h // 2 - 1)]
    names += [("pt", HEADS - 1), ("o", HEADS // 2 - 1)]
    names += [("wo", i) for i in range(4)] + [("up", j) for j in range(MLP_STEPS)]
    names += ["p0", "p1"] + [("proj", i) for i in range(4)] + [("gate", i) for i in range(4)]
    return {n: i for i, n in enumerate(names)}


U2 = units_2()
UNITS2 = len(U2)
assert UNITS1 % WORK == 0 and UNITS2 % WORK == 0


class Signal:

    def __init__(self, sem, one, two, tokens=0, before=0, between=0):
        self.sem, self.tokens = sem, tokens
        self.names = {1: one if isinstance(one, list) else None, 2: two if isinstance(two, list) else None}
        self.per = {1: len(one) if isinstance(one, list) else one, 2: len(two) if isinstance(two, list) else two}
        self.base = {0: 0, 1: before, 15: before + DEPTH * self.per[1]}
        self.base[2] = self.base[15] + between
        self.base[3] = self.base[2] + DEPTH * self.per[2]
        self.made = {1: 0, 2: 0}

    def after(self, here, event):
        block, layer = here
        names = self.names.get(block)
        n = names.index(event) if names is not None and isinstance(event, (str, tuple)) else event
        value = self.tokens + self.base[block] + n + 1
        return layer * self.per[block] + value if block in (1, 2) else value

    def event(self, here, name):
        names = self.names[here[0]]
        assert names[self.made[here[0]]] == name, (name, names[self.made[here[0]]])
        self.made[here[0]] += 1
        return self.sem


def heads_of(name):
    return [(name, h) for h in range(HEADS)]


def build(nc, ins, out):
    with ExitStack() as ctx:
        def sb(name, shape, dt=F32):
            return ctx.enter_context(nc.sbuf_tensor(name, shape, dt))

        def semaphore(name):
            return ctx.enter_context(nc.semaphore(name))

        raw = sb("raw", [P, RING, CH])
        w_hi = sb("w_hi", [P, RING, CH], F32R)
        w_lo = sb("w_lo", [P, RING, CH], F32R)
        h = sb("h", [P, KD, T])
        xh = sb("xh", [P, KD, T], F32R)
        xl = sb("xl", [P, KD, T], F32R)
        consts = sb("consts", [P, C_WIDTH])
        rot_r = sb("rot_r", [P, 2, P], F32R)
        zero_r = sb("zero_r", [P, P], F32R)
        vrow = sb("vrow", [P, P])
        vec = sb("vec", [P, P])
        prow = sb("prow", [P, TB, PLE])
        cs = sb("cs", [P, 4, T])
        std = sb("std", [P, 2, T])
        rstd = sb("rstd", [P, 2, T])
        small = sb("small", [P, 64])
        ka = sb("ka", [P, 2, 3, T], F32R)
        kb = sb("kb", [P, 2, 3, T], F32R)
        vp = sb("vp", [P, 2, TB, 2, 192], F32R)
        pw = sb("pw", [P, 2, P])
        pwh = sb("pwh", [P, 2, P], F32R)
        pwl = sb("pwl", [P, 2, P], F32R)
        fa = sb("fa", [P, 7712])
        ra = sb("ra", [P, 10240], F32R)

        def cut(arena, at, *dims):
            n = 1
            for d in dims:
                n *= d
            v = arena[:, at:at + n]
            if len(dims) == 2:
                v = v.rearrange("p (a b) -> p a b", a=dims[0])
            if len(dims) == 3:
                v = v.rearrange("p (a b c) -> p a b c", a=dims[0], b=dims[1])
            return v

        ident = consts[:, C_ID:C_ID + P]
        ones = consts[:, C_ONES:C_ONES + P]
        mask1 = consts[:, C_MASK:C_MASK + 384]
        rcnt = consts[:, C_RCNT:C_RCNT + 512].rearrange("p (a b) -> p a b", a=2)
        eps_col = consts[:, C_COL + 2:C_COL + 3]
        lneps_col = consts[:, C_COL + 3:C_COL + 4]
        gs, si, us, hid = (cut(fa, i * 1024, 2, 2, T) for i in range(4))
        hh, hl = (cut(ra, i * 1024, 2, 2, T) for i in range(2))
        sq = cut(fa, 4096, KD, T)
        lat = cut(fa, 0, 6, T)
        lat_sq = cut(fa, 2048, 5, T)
        merged = cut(fa, 0, KD, T)
        smla = cut(fa, 2048, KD, T)
        bg = cut(fa, 4096, 4, T)
        cg = cut(fa, 5120, 4, T)
        z = cut(fa, 6144, 4, 258)
        s_sb = cut(fa, 4096, 2, 384)
        p_sb = cut(fa, 4864, 2, 384)
        t1 = fa[:, 5632:5888]
        t2 = fa[:, 5888:6144]
        mt = cut(fa, 4096, NB, 2, T)
        kr1 = fa[:, 7176:7432]
        kr2 = fa[:, 7432:7688]
        lath, latl = cut(ra, 0, 5, T), cut(ra, 1280, 5, T)
        qnh, qnl = cut(ra, 2560, 2, T), cut(ra, 3072, 2, T)
        knh, knl = cut(ra, 3584, 2, T), cut(ra, 4096, 2, T)
        yh, yl = cut(ra, 2560, 4, T), cut(ra, 3584, 4, T)
        vh, vl = cut(ra, 4608, 2, TB, T), cut(ra, 5632, 2, TB, T)
        preh, prel = ra[:, 6656:6912], ra[:, 6912:7168]
        qrh, qrl = ra[:, 7168:7424], ra[:, 7424:7680]
        pth, ptl = cut(ra, 7680, 2, 384), cut(ra, 8448, 2, 384)
        oh, ol = cut(ra, 9216, 2, T), cut(ra, 9728, 2, T)
        krph, krpl = ra[:, 7680:7936], ra[:, 7936:8192]
        pp = cut(fa, 0, KD, T)
        gate = cut(fa, 2048, 4, 2, T)
        ph, pl = cut(ra, 9216, 2, T), cut(ra, 9728, 2, T)
        xr = cut(fa, 0, 2, 2, T)
        r1 = cut(fa, 1024, 2, T)
        r2 = cut(fa, 1536, 2, T)
        av = cut(fa, 2048, 2, T)
        gv = cut(fa, 2560, 2, T)
        yp = cut(fa, 3072, 2, T + PAD2)
        cacc = cut(fa, 3644, 2, T)
        rl = cut(fa, 4156, 3, 512)
        pu, pa_, pb_ = (cut(fa, 4156 + i * 544, 2, T + POOL_PAD) for i in range(3))
        py = cut(fa, 5788, 2, T)
        idx = fa[:, 6300:6684]
        work_a = fa[:, 6684:7068]
        work_b = fa[:, 7068:7452]
        v_sb = cut(fa, 7452, TB, 2, 64)
        ln_t = cut(fa, 2048, 2, T)
        ln_s = cut(fa, 2560, 2, T)
        s2_sb = cut(fa, 0, 2, 384)
        p2_sb = cut(fa, 768, 2, 384)
        ob = cut(fa, 0, KD, T)
        preh2, prel2 = cut(ra, 0, 2, 2, T), cut(ra, 1024, 2, 2, T)
        qih, qil = cut(ra, 2048, 2, 2, T), cut(ra, 3072, 2, 2, T)
        qh, ql = cut(ra, 4096, 4, T), cut(ra, 5120, 4, T)
        pt2h, pt2l = cut(ra, 6144, 2, 384), cut(ra, 6912, 2, 384)
        lyh, lyl = cut(ra, 7680, 2, T), cut(ra, 8192, 2, T)
        pyh, pyl = cut(ra, 8704, 2, T), cut(ra, 9216, 2, T)
        x_sb = cut(fa, 0, TB, D)
        ang = cut(fa, 2304, 4, T)
        ang_t = cut(fa, 3328, 4, T)
        out_sb = cut(fa, 0, TB, D)

        acc = ctx.enter_context(nc.psum_tensor("acc", [P, NB, 512], F32))
        work = ctx.enter_context(nc.psum_tensor("work", [P, WORK, 512], F32))
        sums = acc[:, 0, :].rearrange("p (a t) -> p a t", a=2)

        def bank(unit):
            return work[:, unit % WORK, :]

        def bank2(unit):
            return bank(unit).rearrange("p (a t) -> p a t", a=2)

        raw_full = [semaphore(f"raw_full{i}") for i in range(RING)]
        hi_done = Signal(semaphore("hi_done"), N1, N2)
        lo_done = Signal(semaphore("lo_done"), N1, N2, tokens=RING)
        unit_ready = Signal(semaphore("unit_ready"), UNITS1, UNITS2, before=4)
        unit_taken = Signal(semaphore("unit_taken"), UNITS1, UNITS2, tokens=WORK, before=4)
        acc_step = Signal(semaphore("acc_step"), 2 * (FF_STEPS - 1) + PAIRS - 1, MLP_STEPS - 1)
        acc_done = Signal(semaphore("acc_done"), 3 * NB, NB)
        acc_taken = Signal(semaphore("acc_taken"), 3 * NB, NB, tokens=NB)
        h_new = Signal(semaphore("h_new"), NB, 3 * NB, before=NB, between=NB)
        xh_ready = Signal(semaphore("xh_ready"), 4 * KD, 3 * KD)
        xl_ready = Signal(semaphore("xl_ready"), 4 * KD, 3 * KD)
        sq_ready = Signal(semaphore("sq_ready"), 4 * NB + 1, 4 * NB + 1, between=NB)
        sum_ready = Signal(semaphore("sum_ready"), ["ffn1", "mix", "qkv", "ffn2", "ple"],
                           ["pre", "mean", "var", "mixpost", "mlppre", "mlppost"], between=1)
        std_ready = Signal(semaphore("std_ready"), ["ffn1", "mix", "qkv", "ffn2", "ple"],
                           ["pre", "var", "mixpost", "mlppre", "mlppost"], between=1)
        rstd_ready = Signal(semaphore("rstd_ready"), ["ffn1", "mix", "qkv", "ffn2", "ple"],
                            ["pre", "var", "mixpost", "mlppre", "mlppost"], between=1)
        silu_ready = Signal(semaphore("silu_ready"), 2 * FF_STEPS, 0)
        hid_ready = Signal(semaphore("hid_ready"), 2 * FF_STEPS, MLP_STEPS)
        hh_ready = Signal(semaphore("hh_ready"), 2 * FF_STEPS, MLP_STEPS)
        hl_ready = Signal(semaphore("hl_ready"), 2 * FF_STEPS, MLP_STEPS)
        part_1 = ["krpre", "lat", "kr", "y"]
        for hp in range(PAIRS):
            part_1 += [("qn", hp), ("qr", hp), ("k", hp), ("v", hp), ("rope", hp)]
            if hp:
                part_1 += [("pt0", hp - 1), ("pt1", hp - 1), ("o", hp - 1)]
        part_1 += [("pt0", PAIRS - 1), ("pt1", PAIRS - 1), ("o", PAIRS - 1)]
        part_1 += [("merged", b) for b in range(NB)] + ["p"]
        part_2 = ["poolw", "kipre", ("qipre", 0), "ki", ("qipre", 1), ("qi", 0), ("qipre", 2), ("qi", 1),
                  ("qipre", 3), ("qi", 2), "kpre", "v", ("qi", 3), ("qpre", 0), "k",
                  ("qpre", 1), ("q", 0), ("q", 1), "pooly", "pool", "ly", "pw"]
        for hd in range(HEADS):
            if hd:
                part_2 += [("pt", hd - 1)]
            if hd >= 2 and hd % 2 == 0:
                part_2 += [("o", hd // 2 - 1)]
        part_2 += [("pt", HEADS - 1), ("o", HEADS // 2 - 1), "p0", "p1"]
        part_hi = Signal(semaphore("part_hi"), part_1, part_2)
        part_lo = Signal(semaphore("part_lo"),
                         ["krpre", "lat", "kr", "y"] + [("rope", hp) for hp in range(PAIRS)]
                         + [("merged", b) for b in range(NB)],
                         ["poolw", "kipre", ("qipre", 0), "ki", ("qipre", 1), ("qi", 0), ("qipre", 2), ("qi", 1),
                          ("qipre", 3), ("qi", 2), "kpre", ("qi", 3), ("qpre", 0), "k",
                          ("qpre", 1), ("q", 0), ("q", 1), "pooly", "ly"])
        vec_out = Signal(semaphore("vec_out"),
                         ["latn", "krsum", "y"] + [x for hp in range(PAIRS) for x in
                                                  [("ropesum", hp), ("max", 2 * hp), ("max", 2 * hp + 1),
                                                   ("prob", 2 * hp), ("prob", 2 * hp + 1)]]
                         + [("merged", b) for b in range(NB)],
                         ["kisum", ("qisum", 0), ("qisum", 1), ("qisum", 2), ("qisum", 3), "idx", "ksum",
                          "qsum0", "qsum1", "picked", "pooly", "conv", "centred", "lnorm"]
                         + [x for hd in range(HEADS) for x in ([("max", hd)] + ([("prob", hd - 1)] if hd else []))]
                         + [("prob", HEADS - 1)])
        act_out = Signal(semaphore("act_out"),
                         [("gconv", i) for i in range(4)] + heads_of("exp") + ["gmla"]
                         + [("gate", i) for i in range(4)],
                         [("relu", c, i) for c in range(4) for i in range(3)] + ["gv", "lsilu"]
                         + heads_of("exp") + [("gate", i) for i in range(4)])
        masked = Signal(semaphore("masked"), 0, ["idx", "bias"])
        rows_free = Signal(semaphore("rows_free"), 1, 1, tokens=1)
        vrow_full = semaphore("vrow_full")
        prow_full = semaphore("prow_full")
        pw_full = semaphore("pw_full")
        x_full = semaphore("x_full")
        start_full = semaphore("start_full")
        STEPS = {0: 12, 1: 19, 15: 0, 2: 106}
        start_sin = semaphore("start_sin")
        start_rows = semaphore("start_rows")
        zeroed = semaphore("zeroed")
        slots_free = semaphore("slots_free")
        masks_due = semaphore("masks_due")
        step = semaphore("dve_step")
        stored = semaphore("stored")

        def chunk_shape(block, c):
            return CHUNKS[block][c % len(CHUNKS[block])]

        def permuted(block, c):
            return chunk_shape(block, c)[0] == "w_uq"

        def release(here, c):
            block = here[0]
            if block == 1:
                for f, u, first in ((F1, U1["f1"], 0), (W1 + 4, U1["f2"], FF_STEPS - 1 + PAIRS - 1)):
                    if f <= c < f + 33:
                        if c == f:
                            return unit_ready, u
                        if c == f + 1:
                            return unit_ready, u + 1
                        if c == f + 32:
                            return acc_done, NB - 1 + (0 if f == F1 else 2 * NB)
                        j, kind = divmod(c - f + 1, 3)
                        if kind == 2:
                            return acc_step, first + j - 1
                        return unit_ready, u + 2 * j + kind
                if c < B1:
                    return unit_ready, U1["a"] + c - A1
                if c < B1 + 2:
                    return unit_ready, U1["b"] + c - B1
                if c < C1:
                    return unit_ready, U1["b"] + 1 + c - B1
                if c < D1:
                    return unit_ready, U1["c"] + c - C1
                if c < E1:
                    return unit_ready, U1["d"] + c - D1
                if c < W1:
                    kinds = []
                    for hp in range(PAIRS):
                        kinds += [(unit_ready, UE["qr", hp]), (unit_ready, UE["v", hp]), (unit_ready, UE["gm", hp])]
                        if hp:
                            kinds += [(acc_step, FF_STEPS - 1 + hp - 1)]
                    kinds += [(acc_done, 2 * NB - 1)]
                    return kinds[c - E1]
                if c < W1 + 4:
                    return unit_ready, U1["w"] + c - W1
                if c == G1:
                    return unit_ready, U1["proj"] + 3
                return unit_ready, U1["gate"] + c - G1 - 1
            names = ["wi1", ("qi", 0), ("qi", 1), ("qi", 2), ("qi", 3), "v", ("q", 0), ("q", 1), "a", "g", "pool", "pw"]
            names += [("wo", i) for i in range(4)]
            if c < M2:
                return unit_ready, U2[names[c]]
            if c < G2:
                if c == M2:
                    return unit_ready, U2["up", 0]
                if c == M2 + 31:
                    return acc_done, NB - 1
                j, kind = divmod(c - M2 + 1, 2)
                return (acc_step, j - 1) if kind else (unit_ready, U2["up", j])
            if c < G2 + 2:
                return unit_ready, U2["proj", 2 * (c - G2) + 1]
            return unit_ready, U2["gate", c - G2 - 2]

        block_ctx = ctx.enter_context(nc.Block())

        @block_ctx.sync
        def _(sp):
            sp.dma_start(x_sb, ins["x"][0].rearrange("(b p) d -> p b d", p=P)).then_inc(x_full, 16)

            def load(block, layer, c, waited):
                name, row, tiles, col, cols = CHUNKS[block][c]
                src = ins[name][layer, row:row + tiles * P, col:col + cols].rearrange("(k p) n -> p k n", p=P)
                dst = raw[:, c % RING, 0:tiles * cols].rearrange("p (k n) -> p k n", k=tiles)
                sp.wait_ge(lo_done.sem, waited)
                sp.sem_inc(slots_free, 1)
                sp.dma_start(dst, src).then_inc(raw_full[c % RING], 16)

            def ffn_load(layer, here, f, up, down):
                for g in range(2):
                    load(1, layer, f + g, lo_done.after(here, f + g - RING))
                with sp.Fori(1, FF_STEPS) as j:
                    for kind in range(3):
                        c = f - 1 + kind
                        sp.wait_ge(lo_done.sem, lo_done.after(here, 3 * j + (c - RING)))
                        sp.sem_inc(slots_free, 1)
                        slot = raw[:, c % RING, :]
                        if kind < 2:
                            sp.dma_start(slot.rearrange("p (k n) -> p k n", k=KD),
                                         ins[up][layer, :, bass.ds(j * 256 + kind * F_FF, 256)]
                                         .rearrange("(k p) n -> p k n", p=P)).then_inc(raw_full[c % RING], 16)
                        else:
                            sp.dma_start(slot.rearrange("p (k n) -> p k n", k=2),
                                         ins[down][layer, bass.ds(j * 256 - 256, 256), :]
                                         .rearrange("(k p) n -> p k n", p=P)).then_inc(raw_full[c % RING], 16)
                load(1, layer, f + 32, lo_done.after(here, f + 32 - RING))

            with sp.Fori(0, DEPTH) as layer:
                here = (1, layer)
                ffn_load(layer, here, F1, "ffn1_w_gu", "ffn1_w_down")
                for c in range(A1, W1 + 4):
                    load(1, layer, c, lo_done.after(here, c - RING))
                ffn_load(layer, here, W1 + 4, "ffn2_w_gu", "ffn2_w_down")
                for c in range(G1, N1):
                    load(1, layer, c, lo_done.after(here, c - RING))
            with sp.Fori(0, DEPTH) as layer:
                here = (2, layer)
                for c in range(N2):
                    load(2, layer, c, lo_done.after(here, c - RING))
            end = (3, 0)
            for s in range(RING):
                sp.wait_ge(lo_done.sem, lo_done.after(end, s - RING))
                sp.sem_inc(raw_full[s], 16)
            for b in range(TB):
                sp.wait_ge(unit_taken.sem, unit_taken.after(end, 2 * b + 1))
                sp.dma_start(out[0, b * P:(b + 1) * P, :], out_sb[:, b, :]).then_inc(stored, 16)
            sp.wait_ge(stored, 16 * TB)

        @block_ctx.gpsimd
        def _(gp):
            gp.dma_start(consts[:, :], ins["consts"]).then_inc(start_full, 16)
            for i, name in enumerate(("positions", "positions_2")):
                gp.dma_start(fa[:, 7176 + 256 * i:7432 + 256 * i].bitcast(I32),
                             ins[name].to_broadcast([P, T])).then_inc(start_full, 16)
            gp.memset(vrow[:, :], 0.0).then_inc(start_rows, 1)
            gp.memset(ka[:, :, :, :].bitcast(F32), 0.0)
            gp.memset(kb[:, :, :, :].bitcast(F32), 0.0)
            gp.memset(vp[:, :, :, :, :].bitcast(F32), 0.0)
            gp.memset(pw[:, :, :], 0.0)
            gp.memset(zero_r[:, :].bitcast(F32), 0.0).then_inc(zeroed, 1)
            gp.wait_ge(start_rows, 1)
            gp.wait_ge(zeroed, 1)

            def rows(name, layer, at, n, lead=False):
                src = ins[name][layer]
                src = src.rearrange("(r c) -> r c", c=P) if not lead else src.rearrange("j (r c) -> (j r) c", c=P)
                gp.dma_start(vrow[at:at + n, :], src).then_inc(vrow_full, 16)

            with gp.Fori(0, DEPTH) as layer:
                here = (1, layer)
                gp.wait_ge(rows_free.sem, rows_free.after(here, -1))
                rows("ffn1_norm", layer, V1_FFN1, 8)
                rows("mix_norm", layer, V1_MIX, 8)
                rows("ffn2_norm", layer, V1_FFN2, 8)
                rows("ple_norm", layer, V1_PLE, 8)
                rows("q_norm", layer, V1_QN, 3)
                rows("kv_norm", layer, V1_KVN, 2)
                rows("conv_w", layer, V1_CONV, 12, lead=True)
                gp.dma_start(vrow[V1_FINAL:V1_FINAL + 8, :],
                             ins["final_norm"].rearrange("(r c) -> r c", c=P)).then_inc(vrow_full, 16)
                gp.wait_ge(unit_taken.sem, unit_taken.after(here, U1["p"] + 1 - UNITS1))
                gp.dma_start(prow[:, :, :], ins["p"][layer, 0].rearrange("(b p) d -> p b d", p=P)).then_inc(prow_full, 16)
            with gp.Fori(0, DEPTH) as layer:
                here = (2, layer)
                gp.wait_ge(rows_free.sem, rows_free.after(here, -1))
                rows("norm_mix_pre_2", layer, V2_PRE, 8)
                rows("norm_mix_post_2", layer, V2_MIXPOST, 8)
                rows("norm_mlp_pre_2", layer, V2_MLPPRE, 8)
                rows("norm_mlp_post_2", layer, V2_MLPPOST, 8)
                rows("conv_dw_2", layer, V2_DW, 62, lead=True)
                rows("conv_b_2", layer, V2_CB, 2)
                rows("conv_ln_g_2", layer, V2_LG, 2)
                rows("conv_ln_b_2", layer, V2_LB, 2)
                rows("pool_scale_2", layer, V2_PS, 2)
                gp.wait_ge(part_lo.sem, part_lo.after(here, -part_lo.per[2]))
                for g in range(4):
                    q = 64 * (g % 2)
                    gp.dma_start(pw[q:q + 64, g // 2, q:q + 64], ins["pool_w_2"][layer, g]).then_inc(pw_full, 16)
                gp.wait_ge(unit_taken.sem, unit_taken.after(here, U2["p1"] - UNITS2))
                gp.dma_start(prow[:, :, :], ins["p_2"][layer, 0].rearrange("(b p) d -> p b d", p=P)).then_inc(prow_full, 16)
                gp.wait_ge(vec_out.sem, vec_out.after(here, "idx"))
                gp.sem_inc(masks_due, 1)
                for tb in range(TB):
                    n = P * (tb + 1)
                    last = gp.affine_select(out=work_a[:, P * tb:P * tb + n], in_=idx[:, P * tb:P * tb + n],
                                            pattern=[[-1, n]], compare_op=ALU.is_ge, fill=CAUSAL,
                                            base=P * tb, channel_multiplier=1)
                last.then_inc(masked.event(here, "idx"), 1)
                gp.wait_ge(vec_out.sem, vec_out.after(here, "picked"))
                gp.sem_inc(masks_due, 1)
                for tb in range(TB):
                    n = P * (tb + 1)
                    last = gp.affine_select(out=idx[:, P * tb:P * tb + n], in_=work_b[:, P * tb:P * tb + n],
                                            pattern=[[-1, n]], compare_op=ALU.is_ge, fill=NEG,
                                            base=P * tb, channel_multiplier=1)
                last.then_inc(masked.event(here, "bias"), 1)

        @block_ctx.scalar
        def _(act):
            def split_hi(here, c, steps=0, kind=None):
                if kind is not None:
                    act.wait_ge(kind[0].sem, kind[0].after(here, kind[1]))
                s = c % RING
                n = N1 // RING if here[0] == 1 else N2 // RING
                base = 0 if here[0] == 1 else DEPTH * (N1 // RING)
                act.wait_ge(raw_full[s], (here[1] * n + steps + (base + c // RING + 1)) * 16)
                if permuted(here[0], c):
                    src = raw[:, s, 0:1152].rearrange("p (k h n) -> p k h n", k=3, h=2)
                    dst = w_hi[:, s, 0:1152].rearrange("p (k n) -> p k n", k=3)
                    act.activation(dst[:, :, 0:256].rearrange("p k (h n) -> p k h n", h=2), src[:, :, :, 0:128], ACT.Copy)
                    act.activation(dst[:, :, 256:384].rearrange("p k (h n) -> p k h n", h=2), src[:, :, :, 128:192],
                                   ACT.Copy).then_inc(hi_done.sem, 1)
                    return
                _, _, tiles, _, cols = chunk_shape(here[0], c)
                act.activation(w_hi[:, s, 0:tiles * cols], raw[:, s, 0:tiles * cols], ACT.Copy).then_inc(hi_done.sem, 1)

            def next_hi(here, c):
                split_hi(here, c + RING, kind=release(here, c))

            def norm_hi(here, n, gain, source, squares=True):
                for b in range(NB):
                    s, e = source(b)
                    act.wait_ge(s.sem, s.after(here, e))
                    for k in (2 * b, 2 * b + 1):
                        act.activation(xh[:, k, :], h[:, k, :], ACT.Copy,
                                       scale=1.0 if gain is None else vec[:, gain + k:gain + k + 1]).then_inc(xh_ready.sem, 1)
                if squares:
                    for b in range(NB):
                        act.activation(sq[:, 2 * b:2 * b + 2, :], h[:, 2 * b:2 * b + 2, :], ACT.Square).then_inc(sq_ready.sem, 1)

            def make_std(here, name, n=D, eps=eps_col):
                act.wait_ge(sum_ready.sem, sum_ready.after(here, name))
                act.activation(std[:, 0, :], sums[:, 0, :], ACT.Sqrt, scale=1.0 / n, bias=eps).then_inc(
                    std_ready.event(here, name), 1)

            def hi_of_unit(here, unit, name, dst, src):
                act.wait_ge(unit_ready.sem, unit_ready.after(here, unit))
                act.activation(dst, src, ACT.Copy).then_inc(part_hi.event(here, name), 1)

            def ffn(here, f, u, n, gain, name, source, use):
                e = 0 if use == 0 else FF_STEPS
                norm_hi(here, n, gain, source)
                make_std(here, name)

                def silu(p, j):
                    act.wait_ge(unit_taken.sem, unit_taken.after(here, 2 * j + u))
                    act.activation(si[:, p, :, :], gs[:, p, :, :], ACT.Silu).then_inc(silu_ready.sem, 1)

                def hid_hi(p, j):
                    act.wait_ge(hid_ready.sem, hid_ready.after(here, e + j))
                    act.activation(hh[:, p, :, :], hid[:, p, :, :], ACT.Copy).then_inc(hh_ready.sem, 1)

                next_hi(here, f)
                silu(0, 0)
                next_hi(here, f + 1)
                hid_hi(0, 0)
                with act.Fori(0, (FF_STEPS - 1) // 2) as i:
                    for q in range(2):
                        j = 2 * i + (q + 1)
                        p = (q + 1) % 2
                        split_hi(here, f + 2, steps=j, kind=(unit_ready, 2 * j + u))
                        silu(p, j)
                        split_hi(here, f + 3, steps=j, kind=(unit_ready, 2 * j + (u + 1)))
                        hid_hi(p, j)
                        split_hi(here, f + 4, steps=j, kind=(acc_step, j - 1 + release(here, f + 4)[1]))
                next_hi(here, f + 32)

            act.wait_ge(start_full, 16 * 3)
            act.wait_ge(zeroed, 1)
            act.activation(rot_r[:, 0, :], consts[:, C_R1:C_R1 + P], ACT.Copy)
            act.activation(rot_r[:, 1, :], consts[:, C_R2:C_R2 + P], ACT.Copy).then_inc(start_sin, 1)
            act.wait_ge(step, STEPS[0])
            act.activation(cs[:, :, :], ang, ACT.Sin).then_inc(start_sin, 1)
            for c in range(RING):
                split_hi((1, 0), c)

            with act.Fori(0, DEPTH) as layer:
                here = (1, layer)
                act.wait_ge(unit_taken.sem, unit_taken.after(here, U1["vec"]))
                ffn(here, F1, U1["f1"], 0, V1_FFN1, "ffn1", lambda b: (h_new, b - NB), 0)
                norm_hi(here, 1, V1_MIX, lambda b: (acc_taken, b))
                make_std(here, "mix")
                for i in range(3):
                    next_hi(here, A1 + i)
                act.wait_ge(unit_taken.sem, unit_taken.after(here, U1["a"] + 2))
                act.activation(lat_sq, lat[:, 0:5, :], ACT.Square).then_inc(sq_ready.sem, 1)
                act.activation(krph, lat[:, 5, :], ACT.Copy).then_inc(part_hi.event(here, "krpre"), 1)
                next_hi(here, B1)
                next_hi(here, B1 + 1)
                act.wait_ge(sum_ready.sem, sum_ready.after(here, "qkv"))
                act.activation(std[:, 0, :], sums[:, 0, :], ACT.Sqrt, scale=1.0 / 384, bias=eps_col)
                act.activation(std[:, 1, :], sums[:, 1, :], ACT.Sqrt, scale=1.0 / 256, bias=eps_col).then_inc(
                    std_ready.event(here, "qkv"), 1)
                act.wait_ge(vec_out.sem, vec_out.after(here, "latn"))
                for k in range(5):
                    last = act.activation(lath[:, k, :], lat[:, k, :], ACT.Copy, scale=vec[:, V1_QN + k:V1_QN + k + 1])
                last.then_inc(part_hi.event(here, "lat"), 1)
                act.wait_ge(vec_out.sem, vec_out.after(here, "krsum"))
                act.activation(ka[0:64, 0, 0, :], kr1[0:64, :], ACT.Copy)
                act.activation(kb[64:128, 0, 0, :], kr1[0:64, :], ACT.Copy).then_inc(part_hi.event(here, "kr"), 1)
                for i in range(2, 6):
                    next_hi(here, B1 + i)
                for i in range(4):
                    next_hi(here, C1 + i)
                    if i == 0:
                        act.wait_ge(vec_out.sem, vec_out.after(here, "y"))
                        act.activation(yh, cg, ACT.Copy).then_inc(part_hi.event(here, "y"), 1)
                    act.wait_ge(unit_taken.sem, unit_taken.after(here, U1["c"] + i))
                    act.activation(merged[:, 2 * i:2 * i + 2, :], merged[:, 2 * i:2 * i + 2, :], ACT.Sigmoid).then_inc(
                        act_out.event(here, ("gconv", i)), 1)
                for i in range(4):
                    next_hi(here, D1 + i)
                c = E1

                def after_scores(hp):
                    hi_of_unit(here, UE["pt0", hp], ("pt0", hp), pth[:, 0, :], bank(UE["pt0", hp])[:, 0:384])
                    hi_of_unit(here, UE["pt1", hp], ("pt1", hp), pth[:, 1, :], bank(UE["pt1", hp])[:, 0:384])
                    hi_of_unit(here, UE["o", hp], ("o", hp), oh, bank2(UE["o", hp]))

                for hp in range(PAIRS):
                    next_hi(here, c)
                    hi_of_unit(here, UE["qn", hp], ("qn", hp), qnh, bank2(UE["qn", hp]))
                    hi_of_unit(here, UE["qr", hp], ("qr", hp), preh, bank(UE["qr", hp])[:, 0:T])
                    next_hi(here, c + 1)
                    hi_of_unit(here, UE["k", hp], ("k", hp), knh, bank2(UE["k", hp]))
                    hi_of_unit(here, UE["v", hp], ("v", hp), vh[:, hp % 2, :, :], bank2(UE["v", hp]))
                    act.wait_ge(vec_out.sem, vec_out.after(here, ("ropesum", hp)))
                    act.activation(qrh, t1, ACT.Copy).then_inc(part_hi.event(here, ("rope", hp)), 1)
                    if hp:
                        after_scores(hp - 1)
                    next_hi(here, c + 2)
                    c += 3
                    for hd in range(2):
                        act.wait_ge(vec_out.sem, vec_out.after(here, ("max", 2 * hp + hd)))
                        for tb, (a, n) in enumerate(((0, P), (P, T))):
                            last = act.activation(p_sb[:, hd, a:a + n], s_sb[:, hd, a:a + n], ACT.Exp,
                                                  bias=small[:, 8 + 2 * hd + tb:9 + 2 * hd + tb],
                                                  accum_out=small[:, 16 + 2 * hd + tb:17 + 2 * hd + tb])
                        last.then_inc(act_out.event(here, ("exp", 2 * hp + hd)), 1)
                    if hp:
                        next_hi(here, c)
                        c += 1
                after_scores(PAIRS - 1)
                act.activation(smla, smla, ACT.Sigmoid).then_inc(act_out.event(here, "gmla"), 1)
                next_hi(here, c)
                for b in range(NB):
                    act.wait_ge(vec_out.sem, vec_out.after(here, ("merged", b)))
                    act.activation(xh[:, 2 * b:2 * b + 2, :], merged[:, 2 * b:2 * b + 2, :], ACT.Copy).then_inc(
                        part_hi.event(here, ("merged", b)), 1)
                for i in range(4):
                    next_hi(here, W1 + i)
                ffn(here, W1 + 4, U1["f2"], 2, V1_FFN2, "ffn2", lambda b: (unit_taken, U1["w"] + b), 2)
                hi_of_unit(here, U1["p"], "p", ph[:, :, :], bank2(U1["p"]))
                norm_hi(here, 3, V1_PLE, lambda b: (acc_taken, 2 * NB + b))
                next_hi(here, G1)
                make_std(here, "ple")
                for i in range(4):
                    next_hi(here, G1 + 1 + i)
                    act.wait_ge(unit_taken.sem, unit_taken.after(here, U1["gate"] + i))
                    act.activation(gate[:, i, :, :], gate[:, i, :, :], ACT.Sigmoid).then_inc(
                        act_out.event(here, ("gate", i)), 1)

            mid = (15, 0)
            for b in range(NB):
                act.wait_ge(h_new.sem, h_new.after(mid, b - NB))
                act.activation(sq[:, 2 * b:2 * b + 2, :], h[:, 2 * b:2 * b + 2, :], ACT.Square).then_inc(sq_ready.sem, 1)
            act.wait_ge(sum_ready.sem, sum_ready.after(mid, 0))
            act.activation(std[:, 0, :], sums[:, 0, :], ACT.Sqrt, scale=1.0 / D, bias=eps_col).then_inc(std_ready.sem, 1)

            with act.Fori(0, DEPTH) as layer:
                here = (2, layer)
                act.wait_ge(unit_taken.sem, unit_taken.after(here, U2["vec"]))
                norm_hi(here, 0, V2_PRE, lambda b: (h_new, b - NB))
                make_std(here, "pre")
                act.wait_ge(pw_full, layer * 64 + 64)
                act.activation(pwh[:, :, :], pw[:, :, :], ACT.Copy).then_inc(part_hi.event(here, "poolw"), 1)

                def pre_hi(unit, name, p):
                    act.wait_ge(unit_taken.sem, unit_taken.after(here, U2[unit]))
                    act.activation(preh2[:, p, :, :], xr[:, p, :, :], ACT.Copy).then_inc(part_hi.event(here, name), 1)

                def roped_hi(sum_name, name, dst):
                    act.wait_ge(vec_out.sem, vec_out.after(here, sum_name))
                    act.activation(dst, r1, ACT.Copy).then_inc(part_hi.event(here, name), 1)

                def keys_hi(sum_name, name, slot, src, rows):
                    act.wait_ge(vec_out.sem, vec_out.after(here, sum_name))
                    for i, q in enumerate(rows):
                        act.activation(ka[0:64, 0, slot + i, :], src[q:q + 64, :], ACT.Copy)
                        last = act.activation(kb[64:128, 0, slot + i, :], src[q:q + 64, :], ACT.Copy)
                    last.then_inc(part_hi.event(here, name), 1)

                def relus(c):
                    for i in range(3):
                        act.wait_ge(unit_ready.sem, unit_ready.after(here, U2["dot", c, i]))
                        act.activation(rl[:, i, :], bank(U2["dot", c, i]), ACT.Relu).then_inc(
                            act_out.event(here, ("relu", c, i)), 1)

                next_hi(here, 0)
                act.wait_ge(unit_taken.sem, unit_taken.after(here, U2["ki"]))
                act.activation(preh2[:, 1, 0, :], xr[:, 1, 0, :], ACT.Copy).then_inc(part_hi.event(here, "kipre"), 1)
                next_hi(here, 1)
                pre_hi(("qi", 0), ("qipre", 0), 0)
                keys_hi("kisum", "ki", 2, r1[:, 0, :], (0,))
                for i in range(1, 4):
                    next_hi(here, 1 + i)
                    pre_hi(("qi", i), ("qipre", i), i % 2)
                    roped_hi(("qisum", i - 1), ("qi", i - 1), qih[:, (i - 1) % 2, :, :])
                    relus(i - 1)
                next_hi(here, 5)
                act.wait_ge(unit_taken.sem, unit_taken.after(here, U2["k"]))
                act.activation(preh2[:, 0, 0, :], xr[:, 0, 0, :], ACT.Copy).then_inc(part_hi.event(here, "kpre"), 1)
                act.wait_ge(unit_taken.sem, unit_taken.after(here, U2["v"]))
                act.activation(vp[:, 0, :, :, 64:128], v_sb, ACT.Copy).then_inc(part_hi.event(here, "v"), 1)
                roped_hi(("qisum", 3), ("qi", 3), qih[:, 1, :, :])
                relus(3)
                next_hi(here, 6)
                pre_hi(("q", 0), ("qpre", 0), 1)
                keys_hi("ksum", "k", 0, r1[:, 0, :], (0, 64))
                next_hi(here, 7)
                pre_hi(("q", 1), ("qpre", 1), 0)
                roped_hi("qsum0", ("q", 0), qh[:, 0:2, :])
                next_hi(here, 8)
                roped_hi("qsum1", ("q", 1), qh[:, 2:4, :])
                next_hi(here, 9)
                act.wait_ge(unit_taken.sem, unit_taken.after(here, U2["g"]))
                act.activation(gv, gv, ACT.Sigmoid).then_inc(act_out.event(here, "gv"), 1)
                next_hi(here, 10)
                act.wait_ge(vec_out.sem, vec_out.after(here, "pooly"))
                act.activation(pyh, py, ACT.Copy).then_inc(part_hi.event(here, "pooly"), 1)
                act.wait_ge(unit_ready.sem, unit_ready.after(here, U2["poolw"]))
                for k in range(2):
                    last = act.activation(xh[:, 6 + k, :], bank2(U2["poolw"])[:, k, :], ACT.Copy,
                                          scale=vec[:, V2_PS + k:V2_PS + k + 1])
                last.then_inc(part_hi.event(here, "pool"), 1)
                act.wait_ge(vec_out.sem, vec_out.after(here, "centred"))
                act.activation(ln_s, ln_t, ACT.Square).then_inc(sq_ready.sem, 1)
                make_std(here, "var", 256, lneps_col)
                act.wait_ge(vec_out.sem, vec_out.after(here, "lnorm"))
                for k in range(2):
                    last = act.activation(ln_s[:, k, :], ln_t[:, k, :], ACT.Silu, scale=vec[:, V2_LG + k:V2_LG + k + 1],
                                          bias=vec[:, V2_LB + k:V2_LB + k + 1])
                last.then_inc(act_out.event(here, "lsilu"), 1)
                act.wait_ge(act_out.sem, act_out.after(here, "lsilu"))
                act.activation(lyh, ln_s, ACT.Copy).then_inc(part_hi.event(here, "ly"), 1)
                hi_of_unit(here, U2["pw"], "pw", xh[:, 4:6, :], bank2(U2["pw"]))
                next_hi(here, 11)
                for hd in range(HEADS + 1):
                    if hd < HEADS:
                        act.wait_ge(vec_out.sem, vec_out.after(here, ("max", hd)))
                        for tb, (a, n) in enumerate(((0, P), (P, T))):
                            last = act.activation(p2_sb[:, hd % 2, a:a + n], s2_sb[:, hd % 2, a:a + n], ACT.Exp,
                                                  bias=small[:, 8 + 2 * (hd % 2) + tb:9 + 2 * (hd % 2) + tb],
                                                  accum_out=small[:, 16 + 2 * (hd % 2) + tb:17 + 2 * (hd % 2) + tb])
                        last.then_inc(act_out.event(here, ("exp", hd)), 1)
                    if hd:
                        u = U2["pt", hd - 1]
                        hi_of_unit(here, u, ("pt", hd - 1), pt2h[:, (hd - 1) % 2, :], bank(u)[:, 0:384])
                        if hd % 2 == 0:
                            u = U2["o", hd // 2 - 1]
                            hi_of_unit(here, u, ("o", hd // 2 - 1), xh[:, hd // 2 - 1, :], bank(u)[:, 0:T])
                for i in range(4):
                    next_hi(here, WO2 + i)
                    act.wait_ge(unit_taken.sem, unit_taken.after(here, U2["wo", i]))
                    act.activation(sq[:, 2 * i:2 * i + 2, :], ob[:, 2 * i:2 * i + 2, :], ACT.Square).then_inc(sq_ready.sem, 1)
                make_std(here, "mixpost")
                norm_hi(here, 1, V2_MLPPRE, lambda b: (h_new, b))
                next_hi(here, M2)
                make_std(here, "mlppre")
                for j in range(MLP_STEPS):
                    if j:
                        next_hi(here, M2 + 2 * j - 1)
                    if j >= 2:
                        act.wait_ge(acc_step.sem, acc_step.after(here, j - 2))
                    act.wait_ge(hid_ready.sem, hid_ready.after(here, j))
                    act.activation(hh[:, j % 2, :, :], hid[:, j % 2, :, :], ACT.Copy).then_inc(hh_ready.sem, 1)
                    if j:
                        next_hi(here, M2 + 2 * j)
                next_hi(here, M2 + 31)
                for b in range(NB):
                    act.wait_ge(acc_taken.sem, acc_taken.after(here, b))
                    act.activation(sq[:, 2 * b:2 * b + 2, :], ob[:, 2 * b:2 * b + 2, :], ACT.Square).then_inc(sq_ready.sem, 1)
                make_std(here, "mlppost")
                for k in range(2):
                    hi_of_unit(here, U2[f"p{k}"], f"p{k}", ph[:, k, :], bank(U2[f"p{k}"])[:, 0:T])
                next_hi(here, G2)
                next_hi(here, G2 + 1)
                norm_hi(here, 2, None, lambda b: (h_new, NB + b), squares=False)
                for i in range(4):
                    next_hi(here, G2 + 2 + i)
                    act.activation(gate[:, i, :, :], bank2(U2["gate", i]), ACT.Sigmoid).then_inc(
                        act_out.event(here, ("gate", i)), 1)

        @block_ctx.vector
        def _(v):
            made = {0: 0, 1: 0, 15: 0, 2: 0}
            base = {0: 0, 1: STEPS[0]}
            base[15] = base[1] + DEPTH * STEPS[1]
            base[2] = base[15] + STEPS[15]

            def chain(here, *instructions):
                instructions[-1].then_inc(step, 1)
                made[here[0]] += 1
                value = base[here[0]] + made[here[0]]
                v.wait_ge(step, here[1] * STEPS[here[0]] + value if here[0] in (1, 2) else value)

            def split_lo(here, c, steps=0):
                s = c % RING
                v.wait_ge(hi_done.sem, hi_done.after(here, 3 * steps + c))
                if permuted(here[0], c):
                    src = raw[:, s, 0:1152].rearrange("p (k h n) -> p k h n", k=3, h=2)
                    for a, n, lo in ((0, P, 0), (P, 64, 256)):
                        view = [w[:, s, 0:1152].rearrange("p (k n) -> p k n", k=3)[:, :, lo:lo + 2 * n]
                                .rearrange("p k (h n) -> p k h n", h=2) for w in (w_hi, w_lo)]
                        last = v.tensor_tensor(view[1], src[:, :, :, a:a + n], view[0].bitcast(F32), ALU.subtract)
                    last.then_inc(lo_done.sem, 1)
                    return
                _, _, tiles, _, cols = chunk_shape(here[0], c)
                n = tiles * cols
                v.tensor_tensor(w_lo[:, s, 0:n], raw[:, s, 0:n], w_hi[:, s, 0:n].bitcast(F32),
                                ALU.subtract).then_inc(lo_done.sem, 1)

            def lo_part(here, name, dst, src, hi):
                v.wait_ge(part_hi.sem, part_hi.after(here, name))
                v.tensor_tensor(dst, src, hi.bitcast(F32), ALU.subtract).then_inc(part_lo.event(here, name), 1)

            def lo_of_unit(here, unit, name, dst, src, hi):
                v.wait_ge(part_hi.sem, part_hi.after(here, name))
                v.tensor_tensor(dst, src, hi.bitcast(F32), ALU.subtract).then_inc(unit_taken.sem, 1)

            def ready(here, unit):
                v.wait_ge(unit_ready.sem, unit_ready.after(here, unit))

            def taken(here, unit):
                v.wait_ge(unit_taken.sem, unit_taken.after(here, unit))

            def over(tile, n):
                return tile.rearrange("p (a t) -> p a t", a=1).to_broadcast([tile.shape[0], n, T])

            scale_row = rstd[:, 0, :]

            def norm_lo(here, n, gain):
                for k in range(KD):
                    v.wait_ge(xh_ready.sem, xh_ready.after(here, n * KD + k))
                    if gain is None:
                        v.tensor_tensor(xl[:, k, :], h[:, k, :], xh[:, k, :].bitcast(F32), ALU.subtract).then_inc(xl_ready.sem, 1)
                    else:
                        v.scalar_tensor_tensor(xl[:, k, :], h[:, k, :], vec[:, gain + k:gain + k + 1],
                                               xh[:, k, :].bitcast(F32), ALU.mult, ALU.subtract).then_inc(xl_ready.sem, 1)

            def make_rstd(here, name):
                v.wait_ge(std_ready.sem, std_ready.after(here, name))
                v.reciprocal(rstd[:, 0, :], std[:, 0, :]).then_inc(rstd_ready.event(here, name), 1)
                v.wait_ge(rstd_ready.sem, rstd_ready.after(here, name))

            def scaled(here, unit, dst):
                ready(here, unit)
                v.tensor_tensor(dst, bank2(unit), over(scale_row, 2), ALU.mult).then_inc(unit_taken.sem, 1)

            def ffn(here, f, u, n, gain, name, use):
                e = 0 if use == 0 else FF_STEPS
                norm_lo(here, n, gain)
                make_rstd(here, name)

                def gate_in(p, unit, j):
                    v.wait_ge(unit_ready.sem, unit_ready.after(here, 2 * j + u))
                    v.tensor_tensor(gs[:, p, :, :], bank2(unit), over(scale_row, 2), ALU.mult).then_inc(unit_taken.sem, 1)

                def hidden(p, unit, j):
                    v.wait_ge(unit_ready.sem, unit_ready.after(here, 2 * j + (u + 1)))
                    v.tensor_tensor(us[:, p, :, :], bank2(unit), over(scale_row, 2), ALU.mult).then_inc(unit_taken.sem, 1)
                    v.wait_ge(unit_taken.sem, unit_taken.after(here, 2 * j + (u + 1)))
                    v.wait_ge(silu_ready.sem, silu_ready.after(here, e + j))
                    v.tensor_tensor(hid[:, p, :, :], si[:, p, :, :], us[:, p, :, :], ALU.mult).then_inc(hid_ready.sem, 1)

                def hidden_lo(p, j):
                    v.wait_ge(hh_ready.sem, hh_ready.after(here, e + j))
                    v.tensor_tensor(hl[:, p, :, :], hid[:, p, :, :], hh[:, p, :, :].bitcast(F32),
                                    ALU.subtract).then_inc(hl_ready.sem, 1)

                gate_in(0, u, 0)
                split_lo(here, f + RING)
                hidden(0, u + 1, 0)
                split_lo(here, f + 1 + RING)
                hidden_lo(0, 0)
                with v.Fori(0, (FF_STEPS - 1) // 2) as i:
                    for q in range(2):
                        j = 2 * i + (q + 1)
                        p = (q + 1) % 2
                        gate_in(p, u + 2 * (q + 1), j)
                        split_lo(here, f + 2, steps=j)
                        hidden(p, u + 1 + 2 * (q + 1), j)
                        split_lo(here, f + 3, steps=j)
                        hidden_lo(p, j)
                        split_lo(here, f + 4, steps=j)
                for b in range(NB):
                    v.wait_ge(acc_done.sem, acc_done.after(here, use * NB + b))
                    v.scalar_tensor_tensor(h[:, 2 * b:2 * b + 2, :], acc[:, b, :].rearrange("p (a t) -> p a t", a=2), 0.5,
                                           h[:, 2 * b:2 * b + 2, :], ALU.mult, ALU.add).then_inc(acc_taken.sem, 1)
                split_lo(here, f + 32 + RING)

            def masked_scores(here, unit, slot, s, bias, scale, name):
                ready(here, unit)
                v.scalar_tensor_tensor(s[:, slot, :], bank(unit)[:, 0:384], scale, bias, ALU.mult, ALU.add).then_inc(
                    unit_taken.sem, 1)
                taken(here, unit)
                for tb, (a, n) in enumerate(((0, P), (P, T))):
                    last = v.tensor_reduce(small[:, 8 + 2 * slot + tb:9 + 2 * slot + tb], s[:, slot, a:a + n],
                                           AX_X, ALU.max, negate=True)
                last.then_inc(vec_out.event(here, ("max", name)), 1)

            def normalised(here, slot, p, name):
                v.wait_ge(act_out.sem, act_out.after(here, ("exp", name)))
                chain(here, v.reciprocal(small[:, 20 + 2 * slot:22 + 2 * slot], small[:, 16 + 2 * slot:18 + 2 * slot]))
                for tb, (a, n) in enumerate(((0, P), (P, T))):
                    last = v.tensor_scalar(p[:, slot, a:a + n], p[:, slot, a:a + n],
                                           small[:, 20 + 2 * slot + tb:21 + 2 * slot + tb], None, ALU.mult)
                last.then_inc(vec_out.event(here, ("prob", name)), 1)

            v.sem_inc(lo_done.sem, RING)
            v.sem_inc(unit_taken.sem, WORK)
            v.sem_inc(acc_taken.sem, NB)
            v.sem_inc(rows_free.sem, 1)
            v.wait_ge(zeroed, 1)
            start = (0, 0)
            v.wait_ge(start_full, 16 * 3)
            pos = fa[:, 7176:7688].bitcast(I32)
            chain(start, v.tensor_copy(ang_t[:, 0, :], pos[:, 0:T]), v.tensor_copy(ang_t[:, 1, :], pos[:, T:2 * T]))
            for i in range(2):
                last = v.tensor_scalar(ang[:, 2 * i, :], ang_t[:, i, :], consts[:, C_COL + i:C_COL + i + 1], None, ALU.mult)
            chain(start, last)
            magic = 1.5 * 2.0 ** 23
            both = ang.rearrange("p (a b) t -> p a b t", a=2)
            a0, a1 = both[:, :, 0, :], both[:, :, 1, :]
            turns = ang_t[:, 0:2, :]
            chain(start, v.tensor_scalar(turns, a0, 1.0 / TWO_PI, magic, ALU.mult, ALU.add))
            chain(start, v.tensor_scalar(turns, turns, magic, None, ALU.subtract))
            for part in TWO_PI_PARTS:
                chain(start, v.scalar_tensor_tensor(a0, turns, -part, a0, ALU.mult, ALU.add))
            chain(start, v.tensor_scalar(a1, a0, PI_BELOW, -PI_BELOW, ALU.min, ALU.max))
            chain(start, v.tensor_scalar(a0, a0, TWO_PI / 4, None, ALU.add))
            chain(start, v.tensor_scalar(turns, a0, PI_BELOW, TWO_PI, ALU.is_gt, ALU.mult))
            chain(start, v.tensor_tensor(a0, a0, turns, ALU.subtract))
            chain(start, v.tensor_scalar(a0, a0, PI_BELOW, -PI_BELOW, ALU.min, ALU.max))
            cos1, sin1, cos2, sin2 = (cs[:, i, :] for i in range(4))
            for c in range(RING):
                split_lo((1, 0), c)
            for b in range(NB):
                v.wait_ge(unit_ready.sem, unit_ready.after(start, b))
                v.tensor_copy(h[:, 2 * b:2 * b + 2, :], bank2(b)).then_inc(h_new.sem, 1)
                v.tensor_copy(small[:, b:b + 1], bank(b)[:, 0:1]).then_inc(unit_taken.sem, 1)

            with v.Fori(0, DEPTH) as layer:
                here = (1, layer)
                ready(here, U1["vec"])
                v.tensor_copy(vec[:, :], bank(U1["vec"])[:, 0:P]).then_inc(unit_taken.sem, 1)
                taken(here, U1["vec"])
                v.memset(small[:, 1:2], 0.0).then_inc(rows_free.sem, 1)
                ffn(here, F1, U1["f1"], 0, V1_FFN1, "ffn1", 0)
                norm_lo(here, 1, V1_MIX)
                make_rstd(here, "mix")
                for i in range(3):
                    scaled(here, U1["a"] + i, lat[:, 2 * i:2 * i + 2, :])
                    split_lo(here, A1 + i + RING)
                lo_part(here, "krpre", krpl, lat[:, 5, :], krph)
                v.tensor_tensor(kr1, lat[:, 5, :], cos1, ALU.mult)
                chain(here, v.memset(z[:, :, 0:2], 0.0))
                scaled(here, U1["b"], bg[:, 0:2, :])
                split_lo(here, B1 + RING)
                scaled(here, U1["b"] + 1, bg[:, 2:4, :])
                split_lo(here, B1 + 1 + RING)
                ready(here, U1["b"] + 2)
                v.tensor_tensor(kr2, bank(U1["b"] + 2)[:, 0:T], sin1, ALU.mult).then_inc(unit_taken.sem, 1)
                taken(here, U1["b"] + 2)
                chain(here, v.tensor_tensor(kr1, kr1, kr2, ALU.add))
                v.wait_ge(std_ready.sem, std_ready.after(here, "qkv"))
                v.reciprocal(std[:, 0, :], std[:, 0, :])
                v.reciprocal(rstd[:, 1, :], std[:, 1, :]).then_inc(rstd_ready.event(here, "qkv"), 1)
                v.wait_ge(rstd_ready.sem, rstd_ready.after(here, "qkv"))
                v.tensor_tensor(lat[:, 0:3, :], lat[:, 0:3, :], over(std[:, 0, :], 3), ALU.mult)
                v.tensor_tensor(lat[:, 3:5, :], lat[:, 3:5, :], over(rstd[:, 1, :], 2), ALU.mult).then_inc(
                    vec_out.event(here, "latn"), 1)
                v.tensor_copy(small[:, 0:1], kr1[:, 0:1]).then_inc(vec_out.event(here, "krsum"), 1)
                v.wait_ge(part_hi.sem, part_hi.after(here, "lat"))
                for k in range(5):
                    last = v.scalar_tensor_tensor(latl[:, k, :], lat[:, k, :], vec[:, V1_QN + k:V1_QN + k + 1],
                                                  lath[:, k, :].bitcast(F32), ALU.mult, ALU.subtract)
                last.then_inc(part_lo.event(here, "lat"), 1)
                v.wait_ge(part_hi.sem, part_hi.after(here, "kr"))
                v.tensor_tensor(ka[0:64, 1, 0, :], kr1[0:64, :], ka[0:64, 0, 0, :].bitcast(F32), ALU.subtract)
                v.tensor_tensor(kb[64:128, 1, 0, :], kr1[0:64, :], ka[0:64, 0, 0, :].bitcast(F32), ALU.subtract).then_inc(
                    part_lo.event(here, "kr"), 1)
                for i in range(2, 4):
                    scaled(here, U1["b"] + 1 + i, cg[:, 2 * i - 4:2 * i - 2, :])
                    split_lo(here, B1 + i + RING)
                for i in range(4, 6):
                    t = 2 * i - 8
                    scaled(here, U1["b"] + 1 + i, z[:, t:t + 2, 2:2 + T])
                    taken(here, U1["b"] + 1 + i)
                    chain(here, v.tensor_tensor(z[:, t:t + 2, 2:2 + T], z[:, t:t + 2, 2:2 + T], cg[:, t:t + 2, :], ALU.mult))
                    split_lo(here, B1 + i + RING)
                for j in range(3):
                    for t in range(4):
                        w = vec[:, V1_CONV + 4 * j + t:V1_CONV + 4 * j + t + 1]
                        if j == 0:
                            last = v.tensor_scalar(cg[:, t, :], z[:, t, 0:T], w, None, ALU.mult)
                        else:
                            last = v.scalar_tensor_tensor(cg[:, t, :], z[:, t, j:j + T], w, cg[:, t, :], ALU.mult, ALU.add)
                    chain(here, last)
                v.tensor_tensor(cg, cg, bg, ALU.mult).then_inc(vec_out.event(here, "y"), 1)
                lo_part(here, "y", yl, cg, yh)
                for i in range(4):
                    scaled(here, U1["c"] + i, merged[:, 2 * i:2 * i + 2, :])
                    split_lo(here, C1 + i + RING)
                for i in range(4):
                    ready(here, U1["d"] + i)
                    v.wait_ge(act_out.sem, act_out.after(here, ("gconv", i)))
                    v.tensor_tensor(merged[:, 2 * i:2 * i + 2, :], merged[:, 2 * i:2 * i + 2, :], bank2(U1["d"] + i),
                                    ALU.mult).then_inc(unit_taken.sem, 1)
                    split_lo(here, D1 + i + RING)
                c = E1

                def after_scores(hp):
                    for name, lo, hi in (("pt0", ptl[:, 0, :], pth[:, 0, :]), ("pt1", ptl[:, 1, :], pth[:, 1, :])):
                        u = UE[name, hp]
                        lo_of_unit(here, u, (name, hp), lo, bank(u)[:, 0:384], hi)
                    u = UE["o", hp]
                    lo_of_unit(here, u, ("o", hp), ol, bank2(u), oh)

                for hp in range(PAIRS):
                    u = UE["qn", hp]
                    lo_of_unit(here, u, ("qn", hp), qnl, bank2(u), qnh)
                    u = UE["qr", hp]
                    v.wait_ge(part_hi.sem, part_hi.after(here, ("qr", hp)))
                    v.tensor_tensor(prel, bank(u)[:, 0:T], preh.bitcast(F32), ALU.subtract)
                    v.tensor_tensor(t1, bank(u)[:, 0:T], cos1, ALU.mult).then_inc(unit_taken.sem, 1)
                    split_lo(here, c + RING)
                    u = UE["k", hp]
                    lo_of_unit(here, u, ("k", hp), knl, bank2(u), knh)
                    u = UE["v", hp]
                    lo_of_unit(here, u, ("v", hp), vl[:, hp % 2, :, :], bank2(u), vh[:, hp % 2, :, :])
                    split_lo(here, c + 1 + RING)
                    u = UE["rot", hp]
                    ready(here, u)
                    v.tensor_tensor(t2, bank(u)[:, 0:T], sin1, ALU.mult).then_inc(unit_taken.sem, 1)
                    taken(here, u)
                    v.tensor_tensor(t1, t1, t2, ALU.add).then_inc(vec_out.event(here, ("ropesum", hp)), 1)
                    lo_part(here, ("rope", hp), qrl, t1, qrh)
                    if hp:
                        after_scores(hp - 1)
                    scaled(here, UE["gm", hp], smla[:, 2 * hp:2 * hp + 2, :])
                    split_lo(here, c + 2 + RING)
                    c += 3
                    for hd in range(2):
                        masked_scores(here, UE[f"sc{hd}", hp], hd, s_sb, mask1, SCALE1, 2 * hp + hd)
                    for hd in range(2):
                        normalised(here, hd, p_sb, 2 * hp + hd)
                    if hp:
                        split_lo(here, c + RING)
                        c += 1
                after_scores(PAIRS - 1)
                v.wait_ge(act_out.sem, act_out.after(here, "gmla"))
                for b in range(NB):
                    v.wait_ge(acc_done.sem, acc_done.after(here, NB + b))
                    v.tensor_tensor(mt[:, b, :, :], acc[:, b, :].rearrange("p (a t) -> p a t", a=2),
                                    smla[:, 2 * b:2 * b + 2, :], ALU.mult).then_inc(acc_taken.sem, 1)
                    v.wait_ge(acc_taken.sem, acc_taken.after(here, NB + b))
                    v.tensor_tensor(merged[:, 2 * b:2 * b + 2, :], merged[:, 2 * b:2 * b + 2, :], mt[:, b, :, :],
                                    ALU.add).then_inc(vec_out.event(here, ("merged", b)), 1)
                    lo_part(here, ("merged", b), xl[:, 2 * b:2 * b + 2, :], merged[:, 2 * b:2 * b + 2, :],
                            xh[:, 2 * b:2 * b + 2, :])
                split_lo(here, c + RING)
                for i in range(4):
                    ready(here, U1["w"] + i)
                    v.tensor_tensor(h[:, 2 * i:2 * i + 2, :], h[:, 2 * i:2 * i + 2, :], bank2(U1["w"] + i),
                                    ALU.add).then_inc(unit_taken.sem, 1)
                    split_lo(here, W1 + i + RING)
                ffn(here, W1 + 4, U1["f2"], 2, V1_FFN2, "ffn2", 2)
                lo_of_unit(here, U1["p"], "p", pl[:, :, :], bank2(U1["p"]), ph[:, :, :])
                norm_lo(here, 3, V1_PLE)
                for i in range(4):
                    ready(here, U1["proj"] + i)
                    v.tensor_copy(pp[:, 2 * i:2 * i + 2, :], bank2(U1["proj"] + i)).then_inc(unit_taken.sem, 1)
                split_lo(here, G1 + RING)
                make_rstd(here, "ple")

                def gated(i):
                    v.wait_ge(act_out.sem, act_out.after(here, ("gate", i)))
                    chain(here, v.tensor_tensor(gate[:, i, :, :], gate[:, i, :, :], pp[:, 2 * i:2 * i + 2, :], ALU.mult))
                    v.tensor_tensor(h[:, 2 * i:2 * i + 2, :], h[:, 2 * i:2 * i + 2, :], gate[:, i, :, :],
                                    ALU.add).then_inc(h_new.sem, 1)

                for i in range(4):
                    scaled(here, U1["gate"] + i, gate[:, i, :, :])
                    split_lo(here, G1 + 1 + i + RING)
                    if i:
                        gated(i - 1)
                gated(3)

            mid = (15, 0)
            v.wait_ge(std_ready.sem, std_ready.after(mid, 0))
            v.reciprocal(rstd[:, 0, :], std[:, 0, :]).then_inc(rstd_ready.sem, 1)
            v.wait_ge(rstd_ready.sem, rstd_ready.after(mid, 0))
            for b in range(NB):
                for k in (2 * b, 2 * b + 1):
                    last = v.scalar_tensor_tensor(h[:, k, :], h[:, k, :], vec[:, V1_FINAL + k:V1_FINAL + k + 1],
                                                  scale_row, ALU.mult, ALU.mult)
                last.then_inc(h_new.sem, 1)
            v.wait_ge(h_new.sem, h_new.after(mid, NB - 1))

            with v.Fori(0, DEPTH) as layer:
                here = (2, layer)
                ready(here, U2["vec"])
                v.tensor_copy(vec[:, :], bank(U2["vec"])[:, 0:P]).then_inc(unit_taken.sem, 1)
                taken(here, U2["vec"])
                v.memset(small[:, 1:2], 0.0).then_inc(rows_free.sem, 1)
                norm_lo(here, 0, V2_PRE)
                make_rstd(here, "pre")
                v.wait_ge(part_hi.sem, part_hi.after(here, "poolw"))
                v.tensor_tensor(pwl[:, :, :], pw[:, :, :], pwh[:, :, :].bitcast(F32), ALU.subtract).then_inc(
                    part_lo.event(here, "poolw"), 1)

                def roped(unit, p, n, name, tile=None):
                    u = U2[unit]
                    v.tensor_tensor(r1[:, 0:n, :], xr[:, p, 0:n, :], over(cos2, n), ALU.mult)
                    ready(here, u)
                    v.tensor_tensor(r2[:, 0:n, :], bank2(u)[:, 0:n, :], over(sin2, n), ALU.mult).then_inc(unit_taken.sem, 1)
                    taken(here, u)
                    v.tensor_tensor(r1[:, 0:n, :], r1[:, 0:n, :], r2[:, 0:n, :], ALU.add).then_inc(
                        vec_out.event(here, name), 1)

                def pre(unit, p, name):
                    scaled(here, U2[unit], xr[:, p, :, :])
                    lo_part(here, name, prel2[:, p, :, :], xr[:, p, :, :], preh2[:, p, :, :])

                def keys_lo(name, slot, rows):
                    v.wait_ge(part_hi.sem, part_hi.after(here, name))
                    for i, q in enumerate(rows):
                        hi = (ka, kb)[q // 64][q:q + 64, 0, slot + i, :].bitcast(F32)
                        v.tensor_tensor(ka[0:64, 1, slot + i, :], r1[q:q + 64, 0, :], hi, ALU.subtract)
                        last = v.tensor_tensor(kb[64:128, 1, slot + i, :], r1[q:q + 64, 0, :], hi, ALU.subtract)
                    last.then_inc(part_lo.event(here, name), 1)

                def weighted(c):
                    for i in range(3):
                        v.wait_ge(act_out.sem, act_out.after(here, ("relu", c, i)))
                        n, a, heads = (T, P, 2) if i < 2 else (P, 0, 4)
                        for g in range(heads):
                            hd = 4 * c + (2 * i + g if i < 2 else g)
                            w = small[:, 32 + 16 * (i < 2) + hd:33 + 16 * (i < 2) + hd]
                            src = rl[:, i, g * n:g * n + n]
                            if hd == 0:
                                last = v.tensor_scalar(idx[:, a:a + n], src, w, None, ALU.mult)
                            else:
                                last = v.scalar_tensor_tensor(idx[:, a:a + n], src, w, idx[:, a:a + n], ALU.mult, ALU.add)
                            if g < heads - 1:
                                chain(here, last)
                        last.then_inc(unit_taken.sem, 1)
                        taken(here, U2["dot", c, i])

                ready(here, U2["ki"])
                v.tensor_tensor(xr[:, 1, 0, :], bank(U2["ki"])[:, 0:T], scale_row, ALU.mult).then_inc(unit_taken.sem, 1)
                split_lo(here, RING)
                lo_part(here, "kipre", prel2[:, 1, 0, :], xr[:, 1, 0, :], preh2[:, 1, 0, :])
                for tb in range(TB):
                    ready(here, U2[f"wi{tb}"])
                    v.tensor_scalar(small[:, 32 + 16 * tb:48 + 16 * tb], bank(U2[f"wi{tb}"])[:, 0:16], IDX_SCALE, None,
                                    ALU.mult).then_inc(unit_taken.sem, 1)
                ready(here, U2["rc"])
                for tb in range(TB):
                    last = v.tensor_copy(small[:, 24 + tb:25 + tb], bank(U2["rc"])[:, P * tb:P * tb + 1])
                last.then_inc(unit_taken.sem, 1)
                taken(here, U2["rc"])
                for tb in range(TB):
                    last = v.tensor_scalar(small[:, 32 + 16 * tb:48 + 16 * tb], small[:, 32 + 16 * tb:48 + 16 * tb],
                                           small[:, 24 + tb:25 + tb], None, ALU.mult)
                chain(here, last)
                pre(("qi", 0), 0, ("qipre", 0))
                split_lo(here, 1 + RING)
                roped("rki", 1, 1, "kisum")
                keys_lo("ki", 2, (0,))
                for i in range(1, 4):
                    pre(("qi", i), i % 2, ("qipre", i))
                    split_lo(here, 1 + i + RING)
                    roped(("rqi", i - 1), (i - 1) % 2, 2, ("qisum", i - 1))
                    lo_part(here, ("qi", i - 1), qil[:, (i - 1) % 2, :, :], r1, qih[:, (i - 1) % 2, :, :])
                    weighted(i - 1)
                ready(here, U2["k"])
                v.tensor_tensor(xr[:, 0, 0, :], bank(U2["k"])[:, 0:T], scale_row, ALU.mult).then_inc(unit_taken.sem, 1)
                lo_part(here, "kpre", prel2[:, 0, 0, :], xr[:, 0, 0, :], preh2[:, 0, 0, :])
                ready(here, U2["v"])
                vps = bank(U2["v"])[:, 0:T].rearrange("p (b g n) -> p b g n", b=TB, g=2)
                for tb in range(TB):
                    last = v.tensor_scalar(v_sb[:, tb, :, :], vps[:, tb, :, :], small[:, 24 + tb:25 + tb], None, ALU.mult)
                last.then_inc(unit_taken.sem, 1)
                split_lo(here, 5 + RING)
                roped(("rqi", 3), 1, 2, ("qisum", 3))
                v.wait_ge(part_hi.sem, part_hi.after(here, "v"))
                chain(here, v.tensor_tensor(vp[:, 1, :, :, 64:128], v_sb, vp[:, 0, :, :, 64:128].bitcast(F32), ALU.subtract))
                lo_part(here, ("qi", 3), qil[:, 1, :, :], r1, qih[:, 1, :, :])
                weighted(3)
                v.tensor_copy(small[:, 0:1], idx[:, 0:1]).then_inc(vec_out.event(here, "idx"), 1)
                pre(("q", 0), 1, ("qpre", 0))
                split_lo(here, 6 + RING)
                roped("rk", 0, 1, "ksum")
                keys_lo("k", 0, (0, 64))
                pre(("q", 1), 0, ("qpre", 1))
                split_lo(here, 7 + RING)
                roped(("rq", 0), 1, 2, "qsum0")
                lo_part(here, ("q", 0), ql[:, 0:2, :], r1, qh[:, 0:2, :])
                scaled(here, U2["a"], av)
                split_lo(here, 8 + RING)
                v.wait_ge(part_lo.sem, part_lo.after(here, ("q", 0)))
                roped(("rq", 1), 0, 2, "qsum1")
                lo_part(here, ("q", 1), ql[:, 2:4, :], r1, qh[:, 2:4, :])
                scaled(here, U2["g"], gv)
                split_lo(here, 9 + RING)
                v.wait_ge(masked.sem, masked.after(here, "idx"))
                v.memset(small[:, 62:63], 0.0)
                for tb in range(TB):
                    a, n = P * tb, P * (tb + 1)
                    src, dst = work_a[:, a:a + n], work_b[:, a:a + n]
                    for r in range(TOPK // 8):
                        chain(here, v.max(small[:, 0:8], src))
                        v.memset(small[:, 62:63], 0.0)
                        chain(here, v.match_replace(dst, small[:, 0:8], src, PICKED))
                        v.memset(small[:, 62:63], 0.0)
                        src, dst = dst, src
                for tb in range(TB):
                    a, n = P * tb, P * (tb + 1)
                    last = v.tensor_scalar(work_b[:, a:a + n], work_a[:, a:a + n], PICKED, NEG, ALU.not_equal, ALU.mult)
                last.then_inc(vec_out.event(here, "picked"), 1)
                v.memset(pu[:, :, 0:POOL_PAD], 0.0)
                v.memset(pa_[:, :, 0:POOL_PAD], 0.0)
                v.memset(pb_[:, :, 0:POOL_PAD], 0.0)
                v.memset(yp[:, :, 0:PAD2], 0.0)
                scaled(here, U2["pool"], pu[:, :, POOL_PAD:])
                taken(here, U2["pool"])
                split_lo(here, 10 + RING)

                def doubled(dst, src, by):
                    chain(here, v.tensor_tensor(dst[:, :, POOL_PAD:], src[:, :, POOL_PAD:],
                                                src[:, :, POOL_PAD - by:POOL_PAD + T - by], ALU.add))

                def window(k, rows, src):
                    v.tensor_tensor(py[rows, k, :], src[rows, k, POOL_PAD:], rcnt[rows, k, :], ALU.mult)

                doubled(pa_, pu, 1)
                window(0, slice(0, 64), pa_)
                doubled(pb_, pa_, 2)
                window(0, slice(64, 128), pb_)
                doubled(pa_, pb_, 4)
                window(1, slice(0, 64), pa_)
                doubled(pb_, pa_, 8)
                window(1, slice(64, 128), pb_)
                chain(here, v.memset(small[:, 0:1], 0.0))
                v.tensor_tensor(py, py, pu[:, :, POOL_PAD:], ALU.subtract).then_inc(vec_out.event(here, "pooly"), 1)
                lo_part(here, "pooly", pyl, py, pyh)
                v.wait_ge(act_out.sem, act_out.after(here, "gv"))
                chain(here, v.tensor_tensor(yp[:, :, PAD2:], av, gv, ALU.mult))
                for j in range(CONV_K2):
                    for k in range(2):
                        w = vec[:, V2_DW + 2 * j + k:V2_DW + 2 * j + k + 1]
                        if j == 0:
                            last = v.tensor_scalar(cacc[:, k, :], yp[:, k, 0:T], w, vec[:, V2_CB + k:V2_CB + k + 1],
                                                   ALU.mult, ALU.add)
                        else:
                            last = v.scalar_tensor_tensor(cacc[:, k, :], yp[:, k, j:j + T], w, cacc[:, k, :],
                                                          ALU.mult, ALU.add)
                    if j < CONV_K2 - 1:
                        chain(here, last)
                last.then_inc(vec_out.event(here, "conv"), 1)
                for k in range(2):
                    v.wait_ge(part_hi.sem, part_hi.after(here, "pool"))
                    last = v.scalar_tensor_tensor(xl[:, 6 + k, :], bank2(U2["poolw"])[:, k, :],
                                                  vec[:, V2_PS + k:V2_PS + k + 1], xh[:, 6 + k, :].bitcast(F32),
                                                  ALU.mult, ALU.subtract)
                last.then_inc(unit_taken.sem, 1)
                v.wait_ge(sum_ready.sem, sum_ready.after(here, "mean"))
                v.scalar_tensor_tensor(ln_t, over(sums[:, 0, :], 2), -1.0 / 256, cacc, ALU.mult, ALU.add).then_inc(
                    vec_out.event(here, "centred"), 1)
                make_rstd(here, "var")
                v.tensor_tensor(ln_t, ln_t, over(scale_row, 2), ALU.mult).then_inc(vec_out.event(here, "lnorm"), 1)
                lo_part(here, "ly", lyl, ln_s, lyh)
                lo_of_unit(here, U2["pw"], "pw", xl[:, 4:6, :], bank2(U2["pw"]), xh[:, 4:6, :])
                split_lo(here, 11 + RING)
                v.wait_ge(masked.sem, masked.after(here, "bias"))
                for hd in range(HEADS + 1):
                    if hd < HEADS:
                        masked_scores(here, U2["sc", hd], hd % 2, s2_sb, idx, SCALE2, hd)
                    if hd:
                        normalised(here, (hd - 1) % 2, p2_sb, hd - 1)
                        u = U2["pt", hd - 1]
                        lo_of_unit(here, u, ("pt", hd - 1), pt2l[:, (hd - 1) % 2, :], bank(u)[:, 0:384],
                                   pt2h[:, (hd - 1) % 2, :])
                        if hd % 2 == 0:
                            u = U2["o", hd // 2 - 1]
                            lo_of_unit(here, u, ("o", hd // 2 - 1), xl[:, hd // 2 - 1, :], bank(u)[:, 0:T],
                                       xh[:, hd // 2 - 1, :])

                def post_norm(name, gain):
                    make_rstd(here, name)
                    for b in range(NB):
                        for k in (2 * b, 2 * b + 1):
                            last = v.scalar_tensor_tensor(ob[:, k, :], ob[:, k, :], vec[:, gain + k:gain + k + 1],
                                                          scale_row, ALU.mult, ALU.mult)
                        chain(here, last)
                        v.tensor_tensor(h[:, 2 * b:2 * b + 2, :], h[:, 2 * b:2 * b + 2, :], ob[:, 2 * b:2 * b + 2, :],
                                        ALU.add).then_inc(h_new.sem, 1)

                for i in range(4):
                    ready(here, U2["wo", i])
                    v.tensor_copy(ob[:, 2 * i:2 * i + 2, :], bank2(U2["wo", i])).then_inc(unit_taken.sem, 1)
                    split_lo(here, WO2 + i + RING)
                post_norm("mixpost", V2_MIXPOST)
                norm_lo(here, 1, V2_MLPPRE)
                make_rstd(here, "mlppre")
                for j in range(MLP_STEPS):
                    u = U2["up", j]
                    p = j % 2
                    scaled(here, u, gs[:, p, :, :])
                    taken(here, u)
                    v.scalar_tensor_tensor(hid[:, p, :, :], gs[:, p, :, :], 0.0, gs[:, p, :, :], ALU.max, ALU.mult).then_inc(
                        hid_ready.sem, 1)
                    split_lo(here, M2 + max(2 * j - 1, 0) + RING)
                    v.wait_ge(hh_ready.sem, hh_ready.after(here, j))
                    v.tensor_tensor(hl[:, p, :, :], hid[:, p, :, :], hh[:, p, :, :].bitcast(F32), ALU.subtract).then_inc(
                        hl_ready.sem, 1)
                    if j:
                        split_lo(here, M2 + 2 * j + RING)
                for b in range(NB):
                    v.wait_ge(acc_done.sem, acc_done.after(here, b))
                    v.tensor_copy(ob[:, 2 * b:2 * b + 2, :], acc[:, b, :].rearrange("p (a t) -> p a t", a=2)).then_inc(
                        acc_taken.sem, 1)
                split_lo(here, M2 + 31 + RING)
                post_norm("mlppost", V2_MLPPOST)
                for k in range(2):
                    u = U2[f"p{k}"]
                    lo_of_unit(here, u, f"p{k}", pl[:, k, :], bank(u)[:, 0:T], ph[:, k, :])
                for i in range(4):
                    ready(here, U2["proj", i])
                    v.tensor_copy(pp[:, 2 * i:2 * i + 2, :], bank2(U2["proj", i])).then_inc(unit_taken.sem, 1)
                    if i % 2:
                        split_lo(here, G2 + i // 2 + RING)
                norm_lo(here, 2, None)
                for i in range(4):
                    v.wait_ge(act_out.sem, act_out.after(here, ("gate", i)))
                    v.tensor_tensor(gate[:, i, :, :], gate[:, i, :, :], pp[:, 2 * i:2 * i + 2, :], ALU.mult).then_inc(
                        unit_taken.sem, 1)
                    taken(here, U2["gate", i])
                    v.tensor_tensor(h[:, 2 * i:2 * i + 2, :], h[:, 2 * i:2 * i + 2, :], gate[:, i, :, :],
                                    ALU.add).then_inc(h_new.sem, 1)
                    split_lo(here, G2 + 2 + i + RING)
            end = (3, 0)
            for i in range(2 * TB):
                ready(end, i)
                v.tensor_copy(out_sb[:, i // 2, (i % 2) * 512:(i % 2) * 512 + 512], bank(i)).then_inc(unit_taken.sem, 1)
            assert made == STEPS, made

        @block_ctx.tensor
        def _(pe):
            def free(here, unit, at=0):
                pe.wait_ge(unit_taken.sem, unit_taken.after(here, at + (unit - WORK)))

            def weights(here, c, at=0):
                pe.wait_ge(lo_done.sem, lo_done.after(here, at + c))
                return w_hi[:, c % RING, :], w_lo[:, c % RING, :]

            def product(dst, pairs, start=True, stop=True, group=True):
                for i, ((ah, al), (bh, bl)) in enumerate(pairs):
                    pe.matmul(dst, ah, bh, start=start and i == 0, stop=False, skip_group_check=not group)
                    pe.matmul(dst, ah, bl, start=False, stop=False, skip_group_check=not group)
                    last = pe.matmul(dst, al, bh, start=False, stop=stop and i == len(pairs) - 1,
                                     skip_group_check=not group)
                return last

            def tiles(pair, *index):
                return pair[0][index], pair[1][index]

            def columns(w, at, n=P):
                return w[0][:, at:at + n], w[1][:, at:at + n]

            everything = slice(None)

            def project(here, c, unit, depth=KD, cols=256, x=None, at=0, first=0, n=2, wait_x=None, uat=0):
                x = x or (xh, xl)
                free(here, unit, uat)
                w = weights(here, c, at)
                for m in range(n):
                    pairs = []
                    for k in range(depth):
                        if wait_x is not None and m == 0:
                            pe.wait_ge(xl_ready.sem, xl_ready.after(here, wait_x * KD + k))
                            last = product(bank2(unit)[:, m, :], [(columns(w, k * cols + (first + m) * P), tiles(x, everything, k, everything))],
                                           start=k == 0, stop=k == depth - 1)
                        else:
                            pairs.append((columns(w, k * cols + (first + m) * P), tiles(x, everything, k, everything)))
                    if pairs:
                        last = product(bank2(unit)[:, m, :], pairs)
                last.then_inc(unit_ready.sem, 1)

            def token_major(here, w, unit, depth, cols, at, n, x=None, x0=0, tbs=range(TB), stride=P):
                x = x or (xh, xl)
                free(here, unit)
                for i, tb in enumerate(tbs):
                    last = product(bank(unit)[:, i * stride:i * stride + n],
                                   [(tiles(x, everything, x0 + k, slice(tb * P, tb * P + P)), columns(w, k * cols + at, n))
                                    for k in range(depth)])
                last.then_inc(unit_ready.sem, 1)

            def total(here, name, events, src, first=0, n=KD):
                if events is not None:
                    pe.wait_ge(sq_ready.sem, sq_ready.after(here, events))
                for k in range(n):
                    last = pe.matmul(sums[:, first, :], ones, src[:, k, :], start=k == 0, stop=k == n - 1)
                return last

            def summed(here, name, events, src, n=KD):
                last = total(here, name, events, src, 0, n)
                last.then_inc(sum_ready.event(here, name), 1)

            def open_acc(here, name):
                pe.wait_ge(rstd_ready.sem, rstd_ready.after(here, name))
                for b in range(NB):
                    for a in range(2):
                        pe.matmul(acc[:, b, a * T:a * T + T], zero_r[:, :], rot_r[:, :, :], start=True, stop=True)

            def accumulate(here, c, x, done=None, at=0):
                w = weights(here, c, at)
                for b in range(NB):
                    for a in range(2):
                        last = product(acc[:, b, a * T:a * T + T],
                                       [(columns(w, k * D + (2 * b + a) * P), tiles(x, everything, k, everything))
                                        for k in range(2)], start=False, stop=done is not None, group=False)
                    if done is not None:
                        last.then_inc(acc_done.sem, 1)
                if done is None:
                    last.then_inc(acc_step.sem, 1)

            def hidden(p):
                return hh[:, p, :, :], hl[:, p, :, :]

            def ffn(here, f, u, n, name, squares, use):
                e = 0 if use == 0 else FF_STEPS
                project(here, f, u, wait_x=n)
                summed(here, name, squares, sq)
                open_acc(here, name)
                project(here, f + 1, u + 1)
                with pe.Fori(0, (FF_STEPS - 1) // 2) as i:
                    for q in range(2):
                        project(here, f + 2, u + 2 + 2 * q, at=6 * i + 3 * q, uat=4 * i)
                        project(here, f + 3, u + 3 + 2 * q, at=6 * i + 3 * q, uat=4 * i)
                        pe.wait_ge(hl_ready.sem, hl_ready.after(here, 2 * i + (q + e)))
                        accumulate(here, f + 4, hidden(q), at=6 * i + 3 * q)
                pe.wait_ge(hl_ready.sem, hl_ready.after(here, e + FF_STEPS - 1))
                accumulate(here, f + 32, hidden((FF_STEPS - 1) % 2), done=use)

            def flip(dst, src):
                return pe.transpose(dst, src, ident)

            start = (0, 0)
            pe.wait_ge(start_full, 16 * 3)
            pe.wait_ge(x_full, 16)
            pe.wait_ge(zeroed, 1)
            pe.wait_ge(start_sin, 1)
            for b in range(NB):
                free(start, b)
                for t in range(2):
                    for tb in range(TB):
                        last = flip(bank2(b)[:, t, tb * P:tb * P + P], x_sb[:, tb, (2 * b + t) * P:(2 * b + t) * P + P])
                last.then_inc(unit_ready.sem, 1)

            with pe.Fori(0, DEPTH) as layer:
                here = (1, layer)
                free(here, U1["vec"])
                pe.wait_ge(vrow_full, layer * 128 + 128)
                flip(bank(U1["vec"])[:, 0:P], vrow[:, :]).then_inc(unit_ready.sem, 1)
                ffn(here, F1, U1["f1"], 0, "ffn1", NB - 1, 0)
                project(here, A1, U1["a"], wait_x=1)
                summed(here, "mix", 2 * NB - 1, sq)
                for i in range(1, 3):
                    project(here, A1 + i, U1["a"] + i)
                project(here, B1, U1["b"])
                project(here, B1 + 1, U1["b"] + 1)
                unit = U1["b"] + 2
                free(here, unit)
                pe.wait_ge(part_lo.sem, part_lo.after(here, "krpre"))

                def rotated(dst, which, hi, lo):
                    pe.matmul(dst, rot_r[:, which, :], hi, start=True, stop=False)
                    return pe.matmul(dst, rot_r[:, which, :], lo, start=False, stop=True)

                rotated(bank(unit)[:, 0:T], 0, krph, krpl).then_inc(unit_ready.sem, 1)
                total(here, "qkv", 2 * NB, lat_sq, 0, 3)
                total(here, "qkv", None, lat_sq[:, 3:5, :], 1, 2).then_inc(sum_ready.event(here, "qkv"), 1)
                for i in range(2, 6):
                    project(here, B1 + i, unit - 1 + i)
                for i in range(4):
                    project(here, C1 + i, U1["c"] + i)
                pe.wait_ge(part_lo.sem, part_lo.after(here, "y"))
                for i in range(4):
                    project(here, D1 + i, U1["d"] + i, depth=CONV // P, x=(yh, yl))

                def probs_and_output(hp):
                    for hd in range(2):
                        u = UE[f"pt{hd}", hp]
                        free(here, u)
                        pe.wait_ge(vec_out.sem, vec_out.after(here, ("prob", 2 * hp + hd)))
                        for a in range(3):
                            last = flip(bank(u)[:, a * P:a * P + P], p_sb[:, hd, a * P:a * P + P])
                        last.then_inc(unit_ready.sem, 1)
                    u = UE["o", hp]
                    free(here, u)
                    for hd in range(2):
                        pe.wait_ge(unit_taken.sem, unit_taken.after(here, UE[f"pt{hd}", hp]))
                        values = [(vh[:, hp % 2, kt, hd * P:hd * P + P], vl[:, hp % 2, kt, hd * P:hd * P + P]) for kt in range(TB)]
                        product(bank2(u)[:, hd, :], [(values[0], (pth[:, hd, 0:T], ptl[:, hd, 0:T]))], stop=False)
                        last = product(bank2(u)[:, hd, P:T], [(values[1], (pth[:, hd, T:384], ptl[:, hd, T:384]))], start=False)
                    last.then_inc(unit_ready.sem, 1)

                pe.wait_ge(part_lo.sem, part_lo.after(here, "lat"))
                latent = (lath, latl)
                c = E1
                for hp in range(PAIRS):
                    project(here, c, UE["qn", hp], depth=3, cols=384, x=latent)
                    project(here, c, UE["qr", hp], depth=3, cols=384, x=latent, first=2, n=1)
                    u = UE["k", hp]
                    free(here, u)
                    w = weights(here, c + 1)
                    for hd in range(2):
                        last = product(bank2(u)[:, hd, :],
                                       [(columns(w, k * 512 + hd * 256), tiles(latent, everything, 3 + k, everything))
                                        for k in range(2)])
                    last.then_inc(unit_ready.sem, 1)
                    u = UE["v", hp]
                    free(here, u)
                    for tb in range(TB):
                        last = product(
                            bank2(u)[:, tb, :],
                            [(tiles(latent, everything, 3 + k, slice(tb * P, tb * P + P)),
                              tuple(part[:, k * 512:k * 512 + 512].rearrange("p (h n) -> p h n", h=2)[:, :, P:2 * P] for part in w))
                             for k in range(2)])
                    last.then_inc(unit_ready.sem, 1)
                    u = UE["rot", hp]
                    free(here, u)
                    pe.wait_ge(unit_taken.sem, unit_taken.after(here, UE["qr", hp]))
                    rotated(bank(u)[:, 0:T], 0, preh, prel).then_inc(unit_ready.sem, 1)
                    if hp:
                        probs_and_output(hp - 1)
                    project(here, c + 2, UE["gm", hp])
                    c += 3
                    pe.wait_ge(unit_taken.sem, unit_taken.after(here, UE["k", hp]))
                    pe.wait_ge(part_lo.sem, part_lo.after(here, "kr"))
                    pe.wait_ge(part_lo.sem, part_lo.after(here, ("rope", hp)))
                    for hd in range(2):
                        u = UE[f"sc{hd}", hp]
                        free(here, u)
                        kr = (ka, kb)[hd]
                        for tb, at in ((0, 0), (1, P)):
                            n, queries = P * (tb + 1), slice(tb * P, tb * P + P)
                            last = product(bank(u)[:, at:at + n],
                                           [((qnh[:, hd, queries], qnl[:, hd, queries]), (knh[:, hd, 0:n], knl[:, hd, 0:n])),
                                            ((qrh[:, queries], qrl[:, queries]), (kr[:, 0, 0, 0:n], kr[:, 1, 0, 0:n]))])
                        last.then_inc(unit_ready.sem, 1)
                    if hp:
                        if hp == 1:
                            open_acc(here, "qkv")
                        pe.wait_ge(unit_taken.sem, unit_taken.after(here, UE["o", hp - 1]))
                        accumulate(here, c, (oh, ol))
                        c += 1
                probs_and_output(PAIRS - 1)
                pe.wait_ge(unit_taken.sem, unit_taken.after(here, UE["o", PAIRS - 1]))
                accumulate(here, c, (oh, ol), done=1)
                pe.wait_ge(part_lo.sem, part_lo.after(here, ("merged", NB - 1)))
                for i in range(4):
                    project(here, W1 + i, U1["w"] + i)
                ffn(here, W1 + 4, U1["f2"], 2, "ffn2", 2 * NB + NB, 2)

                def embedding_rows(unit, ks, full):
                    free(here, unit)
                    pe.wait_ge(prow_full, full)
                    for i, k in enumerate(ks):
                        for tb in range(TB):
                            last = flip(bank2(unit)[:, i, tb * P:tb * P + P], prow[:, tb, k * P:k * P + P])
                    last.then_inc(unit_ready.sem, 1)

                embedding_rows(U1["p"], range(2), layer * 16 + 16)
                pe.wait_ge(unit_taken.sem, unit_taken.after(here, U1["p"]))
                for i in range(4):
                    project(here, G1, U1["proj"] + i, depth=2, cols=D, x=(ph, pl), first=2 * i)
                project(here, G1 + 1, U1["gate"], wait_x=3)
                summed(here, "ple", 4 * NB, sq)
                for i in range(1, 4):
                    project(here, G1 + 1 + i, U1["gate"] + i)

            mid = (15, 0)
            total(mid, "final", NB - 1, sq).then_inc(sum_ready.sem, 1)

            with pe.Fori(0, DEPTH) as layer:
                here = (2, layer)
                free(here, U2["vec"])
                pe.wait_ge(vrow_full, layer * 144 + (DEPTH * 128 + 144))
                flip(bank(U2["vec"])[:, 0:P], vrow[:, :]).then_inc(unit_ready.sem, 1)

                project(here, KI2, U2["ki"], n=1, wait_x=0)
                w = weights(here, KI2)
                for tb in range(TB):
                    token_major(here, w, U2[f"wi{tb}"], KD, 256, 64, IDX_HEADS, tbs=(tb,))
                summed(here, "pre", NB - 1, sq)
                u = U2["rc"]
                free(here, u)
                pe.wait_ge(rstd_ready.sem, rstd_ready.after(here, "pre"))
                for tb in range(TB):
                    last = flip(bank(u)[:, tb * P:tb * P + P], rstd[:, 0, tb * P:tb * P + P])
                last.then_inc(unit_ready.sem, 1)

                def rotation(unit, name, p, n):
                    free(here, U2[unit])
                    pe.wait_ge(part_lo.sem, part_lo.after(here, name))
                    rotated(bank2(U2[unit])[:, 0:n, :], 1, preh2[:, p, 0:n, :], prel2[:, p, 0:n, :]).then_inc(
                        unit_ready.sem, 1)

                def dots(c):
                    pe.wait_ge(part_lo.sem, part_lo.after(here, ("qi", c)))
                    for i in range(3):
                        u = U2["dot", c, i]
                        free(here, u)
                        n, queries, heads = (T, slice(P, T), 2) if i < 2 else (P, slice(0, P), 4)
                        for g in range(heads):
                            tile = i if i < 2 else g // 2
                            keys = (ka, kb)[g % 2]
                            last = product(bank(u)[:, g * n:g * n + n],
                                           [((qih[:, c % 2, tile, queries], qil[:, c % 2, tile, queries]),
                                             (keys[:, 0, 2, 0:n], keys[:, 1, 2, 0:n]))])
                        last.then_inc(unit_ready.sem, 1)

                project(here, 1, U2["qi", 0])
                rotation("rki", "kipre", 1, 1)
                for i in range(1, 4):
                    project(here, 1 + i, U2["qi", i])
                    rotation(("rqi", i - 1), ("qipre", i - 1), (i - 1) % 2, 2)
                    dots(i - 1)
                project(here, 5, U2["k"], n=1)
                token_major(here, weights(here, 5), U2["v"], KD, 256, P, P)
                rotation(("rqi", 3), ("qipre", 3), 1, 2)
                dots(3)
                project(here, 6, U2["q", 0])
                rotation("rk", "kpre", 0, 1)
                project(here, 7, U2["q", 1])
                rotation(("rq", 0), ("qpre", 0), 1, 2)
                project(here, 8, U2["a"])
                rotation(("rq", 1), ("qpre", 1), 0, 2)
                project(here, 9, U2["g"])
                project(here, 10, U2["pool"])
                u = U2["poolw"]
                free(here, u)
                pe.wait_ge(part_lo.sem, part_lo.after(here, "poolw"))
                pe.wait_ge(part_lo.sem, part_lo.after(here, "pooly"))
                for k in range(2):
                    last = product(bank2(u)[:, k, :], [((pwh[:, k, :], pwl[:, k, :]), (pyh[:, k, :], pyl[:, k, :]))])
                last.then_inc(unit_ready.sem, 1)
                pe.wait_ge(vec_out.sem, vec_out.after(here, "conv"))
                summed(here, "mean", None, cacc, 2)
                summed(here, "var", NB, ln_s, 2)
                pe.wait_ge(part_lo.sem, part_lo.after(here, "ly"))
                project(here, PW2, U2["pw"], depth=2, x=(lyh, lyl))
                pe.wait_ge(part_lo.sem, part_lo.after(here, ("q", 1)))
                for hd in range(HEADS + 1):
                    if hd < HEADS:
                        u = U2["sc", hd]
                        free(here, u)
                        keys = (ka, kb)[hd % 2]
                        for tb, at in ((0, 0), (1, P)):
                            n, queries = P * (tb + 1), slice(tb * P, tb * P + P)
                            last = product(bank(u)[:, at:at + n],
                                           [((qh[:, hd // 2, queries], ql[:, hd // 2, queries]),
                                             (keys[:, 0, hd // 4, 0:n], keys[:, 1, hd // 4, 0:n]))])
                        last.then_inc(unit_ready.sem, 1)
                    if hd:
                        g = hd - 1
                        u = U2["pt", g]
                        free(here, u)
                        pe.wait_ge(vec_out.sem, vec_out.after(here, ("prob", g)))
                        for a in range(3):
                            last = flip(bank(u)[:, a * P:a * P + P], p2_sb[:, g % 2, a * P:a * P + P])
                        last.then_inc(unit_ready.sem, 1)
                    if hd and hd % 2 == 0:
                        u = U2["o", hd // 2 - 1]
                        free(here, u)
                        pe.wait_ge(unit_taken.sem, unit_taken.after(here, U2["pt", hd - 1]))
                        for g in (hd - 2, hd - 1):
                            half = slice(64, 192) if g % 2 == 0 else slice(0, P)
                            for kt, (a, n) in enumerate(((0, T), (T, P))):
                                last = product(bank(u)[:, kt * P:T],
                                               [((vp[:, 0, kt, g // 4, half], vp[:, 1, kt, g // 4, half]),
                                                 (pt2h[:, g % 2, a:a + n], pt2l[:, g % 2, a:a + n]))],
                                               start=g % 2 == 0 and kt == 0, stop=g % 2 == 1 and kt == 1)
                        last.then_inc(unit_ready.sem, 1)
                pe.wait_ge(unit_taken.sem, unit_taken.after(here, U2["o", HEADS // 2 - 1]))
                for i in range(4):
                    project(here, WO2 + i, U2["wo", i])
                summed(here, "mixpost", NB + 1 + NB - 1, sq)
                project(here, M2, U2["up", 0], wait_x=1)
                summed(here, "mlppre", 2 * NB + 1 + NB - 1, sq)
                open_acc(here, "mlppre")
                for j in range(1, MLP_STEPS):
                    project(here, M2 + 2 * j - 1, U2["up", j])
                    pe.wait_ge(hl_ready.sem, hl_ready.after(here, j - 1))
                    accumulate(here, M2 + 2 * j, hidden((j - 1) % 2))
                pe.wait_ge(hl_ready.sem, hl_ready.after(here, MLP_STEPS - 1))
                accumulate(here, M2 + 2 * MLP_STEPS - 1, hidden((MLP_STEPS - 1) % 2), done=0)
                summed(here, "mlppost", 3 * NB + 1 + NB - 1, sq)
                for k in range(2):
                    u = U2[f"p{k}"]
                    free(here, u)
                    pe.wait_ge(prow_full, layer * 16 + (DEPTH * 16 + 16))
                    for tb in range(TB):
                        last = flip(bank(u)[:, tb * P:tb * P + P], prow[:, tb, k * P:k * P + P])
                    last.then_inc(unit_ready.sem, 1)
                pe.wait_ge(unit_taken.sem, unit_taken.after(here, U2["p1"]))
                for i in range(4):
                    project(here, G2 + i // 2, U2["proj", i], depth=2, cols=512, x=(ph, pl), first=2 * (i % 2))
                project(here, G2 + 2, U2["gate", 0], wait_x=2)
                for i in range(1, 4):
                    project(here, G2 + 2 + i, U2["gate", i])

            end = (3, 0)
            pe.wait_ge(h_new.sem, h_new.after(end, -1))
            for i in range(2 * TB):
                free(end, i)
                for q in range(4):
                    last = flip(bank(i)[:, q * P:q * P + P], h[:, 4 * (i % 2) + q, (i // 2) * P:(i // 2) * P + P])
                last.then_inc(unit_ready.sem, 1)


def constants():
    c = np.zeros((P, C_WIDTH), np.float32)
    c[:, C_ID:C_ID + P] = np.eye(P)
    for at, width, half in ((C_R1, 64, 32), (C_R2, 64, 8)):
        for p in range(P):
            if p % width < half:
                c[p + half, at + p] = -1.0
            elif p % width < 2 * half:
                c[p - half, at + p] = 1.0
    c[:, C_ONES:C_ONES + P] = 1.0
    c[0:64, C_MASK + 64:C_MASK + P] = NEG
    c[0:64, C_MASK + 320:C_MASK + 384] = NEG
    for k in range(2):
        for g in range(2):
            w = 2 ** (2 * k + g + 1)
            c[64 * g:64 * g + 64, C_RCNT + k * T:C_RCNT + k * T + T] = np.float32(1.0) / np.minimum(np.arange(T) + 1, w).astype(np.float32)
    f32 = np.float32
    for p in range(P):
        c[p, C_COL] = f32(10000.0) ** (f32(-2 * (p % 32)) / f32(64))
        if p % 64 < 16:
            c[p, C_COL + 1] = f32(500000.0) ** (f32(-2 * (p % 8)) / f32(16))
    c[:, C_COL + 2] = EPS
    c[:, C_COL + 3] = LN_EPS
    return c


_INS = ["x", "p", "positions", "ffn1_norm", "ffn1_w_gu", "ffn1_w_down", "mix_norm", "w_in", "conv_w", "w_conv_out",
        "q_norm", "kv_norm", "w_uq", "w_ukv", "w_mla_out", "w_o", "ffn2_norm", "ffn2_w_gu", "ffn2_w_down", "ple_norm",
        "w_ple_gate", "w_ple_proj", "final_norm", "p_2", "positions_2", "norm_mix_pre_2", "w_in_2", "conv_dw_2",
        "conv_b_2", "conv_ln_g_2", "conv_ln_b_2", "conv_pw_2", "pool_w_2", "pool_scale_2", "w_out_2",
        "norm_mix_post_2", "norm_mlp_pre_2", "w_up_2", "w_down_2", "norm_mlp_post_2", "ple_proj_2", "ple_gate_2"]


def kernel(**inputs):
    import concourse.bacc as bacc
    from concourse.bass_utils import run_bass_kernel_spmd

    nc = bacc.Bacc("TRN2", target_bir_lowering=False, num_devices=1)
    arrays = {f"in_{name}_dram": np.ascontiguousarray(inputs[name]) for name in _INS}
    arrays["in_consts_dram"] = constants()
    ins = {}
    for name in _INS + ["consts"]:
        a = arrays[f"in_{name}_dram"]
        ins[name] = nc.dram_tensor(f"in_{name}_dram", a.shape, mybir.dt.from_np(a.dtype), kind="ExternalInput").ap()
    out = nc.dram_tensor("out_0_dram", (1, T, D), F32, kind="ExternalOutput").ap()
    build(nc, ins, out)
    r = run_bass_kernel_spmd(nc, [arrays], core_ids=[0])
    return r.results[0]["out_0_dram"]
```
